# Optimizing a Trainium2 kernel written in Bass

```python
import math
import jax, jax.numpy as jnp
from jax import lax
import numpy as np

D_MODEL = 1024
BATCH = 1
SEQ = 256
DEPTH = 2

GRID_W = 64
CTX_LEN = 256
N_DIFF_HEADS = 6
DIFF_HEAD_DIM = 64
DIFF_V_DIM = 2 * DIFF_HEAD_DIM
N_FOURIER_GROUPS = 4
FOURIER_GROUP_DIM = 64
ATTN_QK_W = N_DIFF_HEADS * 2 * DIFF_HEAD_DIM
ATTN_V_W = N_DIFF_HEADS * DIFF_V_DIM
FOURIER_W = N_FOURIER_GROUPS * FOURIER_GROUP_DIM
EVEN_IN_W = 2 * ATTN_QK_W + ATTN_V_W + FOURIER_W
EVEN_MIX_W = ATTN_V_W + FOURIER_W
CONV_K = 3
N_EXPERTS = 16
EC_CAPACITY_FACTOR = 2
D_EXPERT = 1024
ROPE_BASE = 10000.0
Q_BLOCK = 128
EPS = 1e-6
N_EVEN = (DEPTH + 1) // 2
N_ODD = DEPTH // 2


def rmsnorm(x, g):
    xf = x.astype(jnp.float32)
    y = xf * lax.rsqrt(jnp.mean(xf * xf, axis=-1, keepdims=True) + EPS)
    return (y * g.astype(jnp.float32)).astype(x.dtype)

def modulate(x, g, shift, scale):
    return rmsnorm(x, g) * (1 + scale) + shift

def ada_params(cond, w_ada, b_ada):
    m = jax.nn.silu(cond) @ w_ada + b_ada
    return jnp.split(m[..., None, :], 6, axis=-1)

def axial_rope(n, dtype):
    rows = n // GRID_W
    r = jnp.repeat(jnp.arange(rows, dtype=jnp.float32), GRID_W)
    col = jnp.tile(jnp.arange(GRID_W, dtype=jnp.float32), rows)
    n_freq = DIFF_HEAD_DIM // 4
    inv = ROPE_BASE ** (-jnp.arange(n_freq, dtype=jnp.float32) / n_freq)
    ar = r[:, None] * inv
    ac = col[:, None] * inv
    ang = jnp.concatenate([ar, ar, ac, ac], axis=-1)
    return jnp.cos(ang).astype(dtype), jnp.sin(ang).astype(dtype)

def apply_rope(x, cos, sin):
    x1, x2, x3, x4 = jnp.split(x, 4, axis=-1)
    rot = jnp.concatenate([-x2, x1, -x4, x3], axis=-1)
    return x * cos[None, :, None, None, :] + rot * sin[None, :, None, None, :]

def qk_heads(t):
    return t.reshape(t.shape[0], t.shape[1], N_DIFF_HEADS, 2, DIFF_HEAD_DIM)

def v_heads(t):
    return t.reshape(t.shape[0], t.shape[1], N_DIFF_HEADS, DIFF_V_DIM)

def diff_attend(q, k, v, lam):
    s = jnp.einsum('bqhmd,bkhmd->bhmqk', q, k).astype(jnp.float32)
    p = jax.nn.softmax(s, axis=-1)
    a = p[:, :, 0] - lam * p[:, :, 1]
    return jnp.einsum('bhqk,bkhe->bqhe', a.astype(v.dtype), v)

def blocked_diff_attend(q, k, v, lam):
    b, n = q.shape[0], q.shape[1]
    qb = q.reshape(b, n // Q_BLOCK, Q_BLOCK, N_DIFF_HEADS, 2, DIFF_HEAD_DIM).swapaxes(0, 1)
    out = lax.map(lambda qq: diff_attend(qq, k, v, lam), qb)
    return out.swapaxes(0, 1).reshape(b, n, N_DIFF_HEADS, DIFF_V_DIM)

def fourier_mix(f):
    b, n = f.shape[0], f.shape[1]
    fg = f.reshape(b, n, N_FOURIER_GROUPS, FOURIER_GROUP_DIM).astype(jnp.float32)
    y = jnp.fft.fft2(fg, axes=(1, 3), norm='ortho').real
    return y.reshape(b, n, FOURIER_W).astype(f.dtype)

def merge_even(att, f, subln, lam_init, w_out):
    b, n = att.shape[0], att.shape[1]
    att = rmsnorm(att, subln) * (1.0 - lam_init)
    o = jnp.concatenate([att.reshape(b, n, ATTN_V_W), fourier_mix(f)], axis=-1)
    return o @ w_out

def even_mixer(h, hc, w_in, q_norm, k_norm, lam, subln, w_out, lam_init, cos, sin, ctx_out):
    scale = DIFF_HEAD_DIM ** -0.5
    cuts = [ATTN_QK_W, 2 * ATTN_QK_W, 2 * ATTN_QK_W + ATTN_V_W]
    q, k, v, f = jnp.split(h @ w_in, cuts, axis=-1)
    q = apply_rope(rmsnorm(qk_heads(q), q_norm), cos, sin) * scale
    k = apply_rope(rmsnorm(qk_heads(k), k_norm), cos, sin)
    qc = None
    fc = None
    if ctx_out:
        qc, kc, vc, fc = jnp.split(hc @ w_in, cuts, axis=-1)
    else:
        kc, vc = jnp.split(hc @ w_in[:, ATTN_QK_W:2 * ATTN_QK_W + ATTN_V_W], [ATTN_QK_W], axis=-1)
    kc = rmsnorm(qk_heads(kc), k_norm)
    vc = v_heads(vc)
    keys = jnp.concatenate([k, kc], axis=1)
    vals = jnp.concatenate([v_heads(v), vc], axis=1)
    y = merge_even(blocked_diff_attend(q, keys, vals, lam), f, subln, lam_init, w_out)
    yc = None
    if ctx_out:
        qc = rmsnorm(qk_heads(qc), q_norm) * scale
        yc = merge_even(diff_attend(qc, kc, vc, lam), fc, subln, lam_init, w_out)
    return y, yc

def shortconv(z, w):
    zp = jnp.pad(z, ((0, 0), (1, 1), (0, 0)))
    return w[0] * zp[:, :-2] + w[1] * zp[:, 1:-1] + w[2] * zp[:, 2:]

def odd_mixer(h, w_in, conv_w, w_out):
    bg, cg, u = jnp.split(h @ w_in, 3, axis=-1)
    return (bg * shortconv(cg * u, conv_w)) @ w_out

def ec_moe(h, w_router, w_gate, w_up, w_down):
    b, n, d = h.shape
    cap = EC_CAPACITY_FACTOR * n // N_EXPERTS
    aff = jax.nn.softmax(h.astype(jnp.float32) @ w_router.astype(jnp.float32), axis=-1)
    g, idx = lax.top_k(aff.swapaxes(1, 2), cap)
    xs = jax.vmap(lambda hb, ib: hb[ib])(h, idx)
    a = jax.nn.silu(jnp.einsum('becd,edf->becf', xs, w_gate)) * jnp.einsum('becd,edf->becf', xs, w_up)
    y = jnp.einsum('becf,efd->becd', a, w_down) * g[..., None].astype(h.dtype)
    return jax.vmap(lambda yb, ib: jnp.zeros((n, d), yb.dtype).at[ib.reshape(-1)].add(yb.reshape(-1, d)))(y, idx)

def first_inputs(seed: int = 0) -> dict:
    key = jax.random.key(seed)
    ks = jax.random.split(key, 24)

    def nrm(k, shape, s):
        return jax.random.normal(k, shape, jnp.float32) * s

    D = D_MODEL
    return {
        'x': nrm(ks[0], (BATCH, SEQ, D), 1.0),
        'c': nrm(ks[1], (BATCH, D), 1.0),
        'ctx': nrm(ks[2], (BATCH, CTX_LEN, D), 1.0),
        'c_ctx': nrm(ks[3], (D,), 1.0),
        'ada_w': nrm(ks[4], (DEPTH, D, 6 * D), 0.5 * D ** -0.5),
        'ada_b': nrm(ks[5], (DEPTH, 6 * D), 0.02),
        'norm_mix': 1.0 + nrm(ks[6], (DEPTH, D), 0.02),
        'norm_ffn': 1.0 + nrm(ks[7], (DEPTH, D), 0.02),
        'attn_w_in': nrm(ks[8], (N_EVEN, D, EVEN_IN_W), D ** -0.5),
        'attn_q_norm': 1.0 + nrm(ks[9], (N_EVEN, DIFF_HEAD_DIM), 0.02),
        'attn_k_norm': 1.0 + nrm(ks[10], (N_EVEN, DIFF_HEAD_DIM), 0.02),
        'lam_q1': nrm(ks[11], (N_EVEN, DIFF_HEAD_DIM), 0.1),
        'lam_k1': nrm(ks[12], (N_EVEN, DIFF_HEAD_DIM), 0.1),
        'lam_q2': nrm(ks[13], (N_EVEN, DIFF_HEAD_DIM), 0.1),
        'lam_k2': nrm(ks[14], (N_EVEN, DIFF_HEAD_DIM), 0.1),
        'attn_subln': 1.0 + nrm(ks[15], (N_EVEN, DIFF_V_DIM), 0.02),
        'attn_w_out': nrm(ks[16], (N_EVEN, EVEN_MIX_W, D), EVEN_MIX_W ** -0.5),
        'conv_w_in': nrm(ks[17], (N_ODD, D, 3 * D), D ** -0.5),
        'conv_w': nrm(ks[18], (N_ODD, CONV_K, D), CONV_K ** -0.5),
        'conv_w_out': nrm(ks[19], (N_ODD, D, D), D ** -0.5),
        'router_w': nrm(ks[20], (DEPTH, D, N_EXPERTS), D ** -0.5),
        'moe_w_gate': nrm(ks[21], (DEPTH, N_EXPERTS, D, D_EXPERT), D ** -0.5),
        'moe_w_up': nrm(ks[22], (DEPTH, N_EXPERTS, D, D_EXPERT), D ** -0.5),
        'moe_w_down': nrm(ks[23], (DEPTH, N_EXPERTS, D_EXPERT, D), D_EXPERT ** -0.5),
    }

def first_block(x, c, ctx, c_ctx, ada_w, ada_b, norm_mix, norm_ffn,
              attn_w_in, attn_q_norm, attn_k_norm, lam_q1, lam_k1, lam_q2, lam_k2,
              attn_subln, attn_w_out, conv_w_in, conv_w, conv_w_out,
              router_w, moe_w_gate, moe_w_up, moe_w_down):
    cos, sin = axial_rope(x.shape[1], x.dtype)
    xc = ctx
    for l in range(DEPTH):
        ctx_out = any(j % 2 == 0 for j in range(l + 1, DEPTH))
        ctx_in = (l % 2 == 0) or ctx_out
        sh_m, sc_m, g_m, sh_f, sc_f, g_f = ada_params(c, ada_w[l], ada_b[l])
        h = modulate(x, norm_mix[l], sh_m, sc_m)
        hc = None
        cg_m = cg_f = csh_f = csc_f = None
        if ctx_in:
            csh_m, csc_m, cg_m, csh_f, csc_f, cg_f = ada_params(c_ctx, ada_w[l], ada_b[l])
            hc = modulate(xc, norm_mix[l], csh_m, csc_m)
        if l % 2 == 0:
            e = l // 2
            lam_init = 0.8 - 0.6 * math.exp(-0.3 * l)
            lam = (jnp.exp(jnp.sum(lam_q1[e].astype(jnp.float32) * lam_k1[e].astype(jnp.float32)))
                   - jnp.exp(jnp.sum(lam_q2[e].astype(jnp.float32) * lam_k2[e].astype(jnp.float32)))
                   + lam_init)
            y, yc = even_mixer(h, hc, attn_w_in[e], attn_q_norm[e], attn_k_norm[e], lam,
                               attn_subln[e], attn_w_out[e], lam_init, cos, sin, ctx_out)
        else:
            o = l // 2
            y = odd_mixer(h, conv_w_in[o], conv_w[o], conv_w_out[o])
            yc = odd_mixer(hc, conv_w_in[o], conv_w[o], conv_w_out[o]) if ctx_out else None
        x = x + g_m * y
        x = x + g_f * ec_moe(modulate(x, norm_ffn[l], sh_f, sc_f),
                             router_w[l], moe_w_gate[l], moe_w_up[l], moe_w_down[l])
        if ctx_out:
            xc = xc + cg_m * yc
            xc = xc + cg_f * ec_moe(modulate(xc, norm_ffn[l], csh_f, csc_f),
                                    router_w[l], moe_w_gate[l], moe_w_up[l], moe_w_down[l])
    return x


DEPTH_2 = 1

N_MEM = 256
MIX_WIDTH = D_MODEL
M_HEADS = 4
M_WIDTH = MIX_WIDTH // 2
M_DV = M_WIDTH // M_HEADS
M_DK = M_DV // 2
CONV_K_2 = 4
CHUNK = 64
F_BIAS_LO = 3.0
F_BIAS_HI = 6.0
A_HEADS = 4
A_DV = 128
A_WIDTH = A_HEADS * A_DV
Q_LORA = 256
KV_LORA = 128
NOPE_DIM = 128
ROPE_DIM = 64
A_QK = NOPE_DIM + ROPE_DIM
ROPE_THETA = 10000.0
IN_SPLITS = (M_WIDTH, M_WIDTH, M_WIDTH, M_HEADS, M_HEADS, Q_LORA, KV_LORA, ROPE_DIM)
IN_COLS = sum(IN_SPLITS)
X_HEADS = 4
X_HD = 128
X_WIDTH = X_HEADS * X_HD
D_FF = 4 * D_MODEL


def rmsnorm_2(x, g):
    xf = x.astype(jnp.float32)
    y = xf * lax.rsqrt(jnp.mean(xf * xf, axis=-1, keepdims=True) + EPS)
    return (y * g.astype(jnp.float32)).astype(x.dtype)

def rope_tables(positions):
    inv = 1.0 / (ROPE_THETA ** (jnp.arange(0, ROPE_DIM, 2, dtype=jnp.float32) / ROPE_DIM))
    ang = positions.astype(jnp.float32)[..., None] * inv
    return jnp.cos(ang), jnp.sin(ang)

def apply_rope_2(x, cos, sin):
    extra = x.ndim - 3
    shp = cos.shape[:2] + (1,) * extra + cos.shape[-1:]
    c = cos.reshape(shp)
    s = sin.reshape(shp)
    x1, x2 = jnp.split(x.astype(jnp.float32), 2, axis=-1)
    return jnp.concatenate([x1 * c - x2 * s, x2 * c + x1 * s], axis=-1).astype(x.dtype)

def causal_dwconv(u, w, b):
    C = u.shape[-1]
    y = lax.conv_general_dilated(
        u, w[:, None, :].astype(u.dtype), window_strides=(1,),
        padding=[(CONV_K_2 - 1, 0)], dimension_numbers=('NWC', 'WIO', 'NWC'),
        feature_group_count=C)
    return y + b

def mlstm_chunkwise(q, k, v, ig, fg):
    f32 = jnp.float32
    Bn, H, S, DK = q.shape
    DV = v.shape[-1]
    L = CHUNK
    NC = S // L
    qc = (q.astype(f32) * (DK ** -0.5)).reshape(Bn, H, NC, L, DK)
    kc = k.astype(f32).reshape(Bn, H, NC, L, DK)
    vc = v.astype(f32).reshape(Bn, H, NC, L, DV)
    logf = jax.nn.log_sigmoid(fg.astype(f32)).reshape(Bn, H, NC, L)
    ic = ig.astype(f32).reshape(Bn, H, NC, L)
    b = jnp.cumsum(logf, axis=-1)
    b_tot = b[..., -1]

    a = b_tot[..., None] - b + ic
    m_loc = jnp.max(a, axis=-1)
    wa = jnp.exp(a - m_loc[..., None])
    C_loc = jnp.einsum('bhcl,bhcld,bhcle->bhcde', wa, kc, vc)
    n_loc = jnp.einsum('bhcl,bhcld->bhcd', wa, kc)

    def step(carry, inp):
        C, n, m = carry
        bt, ml, Cl, nl = inp
        m_new = jnp.maximum(bt + m, ml)
        s_old = jnp.exp(bt + m - m_new)
        s_loc = jnp.exp(ml - m_new)
        C_new = s_old[..., None, None] * C + s_loc[..., None, None] * Cl
        n_new = s_old[..., None] * n + s_loc[..., None] * nl
        return (C_new, n_new, m_new), (C, n, m)

    init = (jnp.zeros((Bn, H, DK, DV), f32), jnp.zeros((Bn, H, DK), f32), jnp.zeros((Bn, H), f32))
    xs = (jnp.moveaxis(b_tot, 2, 0), jnp.moveaxis(m_loc, 2, 0),
          jnp.moveaxis(C_loc, 2, 0), jnp.moveaxis(n_loc, 2, 0))
    _, (C_prev, n_prev, m_prev) = lax.scan(step, init, xs)
    C_prev = jnp.moveaxis(C_prev, 0, 2)
    n_prev = jnp.moveaxis(n_prev, 0, 2)
    m_prev = jnp.moveaxis(m_prev, 0, 2)

    causal = jnp.tril(jnp.ones((L, L), dtype=bool))
    Dlog = b[..., :, None] - b[..., None, :] + ic[..., None, :]
    Dlog = jnp.where(causal, Dlog, -jnp.inf)
    inter_log = b + m_prev[..., None]
    m_j = jnp.maximum(inter_log, jnp.max(Dlog, axis=-1))
    Dw = jnp.exp(Dlog - m_j[..., None])
    qk = jnp.einsum('bhcjd,bhcsd->bhcjs', qc, kc) * Dw
    s_inter = jnp.exp(inter_log - m_j)
    num = (s_inter[..., None] * jnp.einsum('bhcjd,bhcde->bhcje', qc, C_prev)
           + jnp.einsum('bhcjs,bhcse->bhcje', qk, vc))
    den = s_inter * jnp.einsum('bhcjd,bhcd->bhcj', qc, n_prev) + jnp.sum(qk, axis=-1)
    h = num / jnp.maximum(jnp.abs(den), jnp.exp(-m_j))[..., None]
    return h.reshape(Bn, H, S, DV).astype(v.dtype)

def causal_block_attention(q, k, v):
    Bn, H, S, Dq = q.shape
    Dv = v.shape[-1]
    nb = S // Q_BLOCK
    scale = Dq ** -0.5
    qb = q.reshape(Bn, H, nb, Q_BLOCK, Dq).transpose(2, 0, 1, 3, 4)
    kpos = jnp.arange(S)

    def one_block(args):
        qi, bi = args
        s = jnp.einsum('bhqd,bhkd->bhqk', qi, k).astype(jnp.float32) * scale
        qpos = bi * Q_BLOCK + jnp.arange(Q_BLOCK)
        s = jnp.where(kpos[None, :] <= qpos[:, None], s, -jnp.inf)
        p = jax.nn.softmax(s, axis=-1)
        return jnp.einsum('bhqk,bhkd->bhqd', p.astype(v.dtype), v)

    out = lax.map(one_block, (qb, jnp.arange(nb)))
    return out.transpose(1, 2, 0, 3, 4).reshape(Bn, H, S, Dv)

def parallel_mixer(h, cos, sin, w_in, conv_w, conv_b, wq_m, wk_m, b_igate, b_fgate, m_out_g,
                   cq_norm_g, ckv_norm_g, w_uq, w_ukv, qk_norm_q, qk_norm_k, a_out_g, w_out):
    Bn, S, _ = h.shape
    proj = h @ w_in
    idx = np.cumsum(IN_SPLITS)[:-1].tolist()
    u, v_m, o_pre, i_pre, f_pre, c_q, c_kv, k_r = jnp.split(proj, idx, axis=-1)

    u_c = jax.nn.silu(causal_dwconv(u, conv_w, conv_b))
    u_h = u_c.reshape(Bn, S, M_HEADS, M_DV)
    q_m = jnp.einsum('bshd,hde->bhse', u_h, wq_m)
    k_m = jnp.einsum('bshd,hde->bhse', u_h, wk_m)
    v_h = v_m.reshape(Bn, S, M_HEADS, M_DV).transpose(0, 2, 1, 3)
    ig = (i_pre + b_igate).transpose(0, 2, 1)
    fg = (f_pre + b_fgate).transpose(0, 2, 1)
    hm = mlstm_chunkwise(q_m, k_m, v_h, ig, fg)
    hm = rmsnorm_2(hm.transpose(0, 2, 1, 3), m_out_g)
    y_m = jax.nn.sigmoid(o_pre) * hm.reshape(Bn, S, M_WIDTH)

    q_a = (rmsnorm_2(c_q, cq_norm_g) @ w_uq).reshape(Bn, S, A_HEADS, A_QK)
    kv = (rmsnorm_2(c_kv, ckv_norm_g) @ w_ukv).reshape(Bn, S, A_HEADS, NOPE_DIM + A_DV)
    k_nope, v_a = jnp.split(kv, [NOPE_DIM], axis=-1)
    q_nope = rmsnorm_2(q_a[..., :NOPE_DIM], qk_norm_q[:NOPE_DIM])
    q_rope = apply_rope_2(rmsnorm_2(q_a[..., NOPE_DIM:], qk_norm_q[NOPE_DIM:]), cos, sin)
    k_nope = rmsnorm_2(k_nope, qk_norm_k[:NOPE_DIM])
    k_rope = apply_rope_2(rmsnorm_2(k_r, qk_norm_k[NOPE_DIM:]), cos, sin)
    k_rope = jnp.broadcast_to(k_rope[:, :, None, :], (Bn, S, A_HEADS, ROPE_DIM))
    q_full = jnp.concatenate([q_nope, q_rope], axis=-1).transpose(0, 2, 1, 3)
    k_full = jnp.concatenate([k_nope, k_rope], axis=-1).transpose(0, 2, 1, 3)
    o_a = causal_block_attention(q_full, k_full, v_a.transpose(0, 2, 1, 3))
    y_a = rmsnorm_2(o_a.transpose(0, 2, 1, 3), a_out_g).reshape(Bn, S, A_WIDTH)

    return jnp.concatenate([y_m, y_a], axis=-1) @ w_out

def memory_cross_attention(h, mem_n, wq_x, wkv_x, xq_norm_g, xk_norm_g, wo_x):
    Bn, S, _ = h.shape
    Nm = mem_n.shape[1]
    q = rmsnorm_2((h @ wq_x).reshape(Bn, S, X_HEADS, X_HD), xq_norm_g)
    kv = (mem_n @ wkv_x).reshape(Bn, Nm, 2, X_HEADS, X_HD)
    k = rmsnorm_2(kv[:, :, 0], xk_norm_g)
    v = kv[:, :, 1]
    s = jnp.einsum('bshd,bnhd->bhsn', q, k).astype(jnp.float32) * (X_HD ** -0.5)
    p = jax.nn.softmax(s, axis=-1)
    o = jnp.einsum('bhsn,bnhd->bshd', p.astype(v.dtype), v).reshape(Bn, S, X_WIDTH)
    return o @ wo_x

def second_inputs(seed: int = 0) -> dict:
    key = jax.random.key(seed)
    ks = jax.random.split(key, 32)
    f32 = jnp.float32
    nrm = lambda k, shp, scale: jax.random.normal(k, shp, f32) * scale
    gain = lambda k, shp: 1.0 + 0.02 * jax.random.normal(k, shp, f32)
    Ld = DEPTH_2
    x = jax.random.normal(ks[0], (BATCH, SEQ, D_MODEL), f32)
    mem = jax.random.normal(ks[1], (BATCH, N_MEM, D_MODEL), f32)
    offset = jax.random.randint(ks[2], (BATCH, 1), 0, 1024, dtype=jnp.int32)
    positions = (offset + jnp.arange(SEQ, dtype=jnp.int32)[None, :]).astype(jnp.int32)
    b_f = (jnp.linspace(F_BIAS_LO, F_BIAS_HI, M_HEADS, dtype=f32)[None, :]
           + 0.1 * jax.random.normal(ks[10], (Ld, M_HEADS), f32))
    return {
        "x": x,
        "mem": mem,
        "positions": positions,
        "norm_mix_g": gain(ks[3], (Ld, D_MODEL)),
        "w_in": nrm(ks[4], (Ld, D_MODEL, IN_COLS), D_MODEL ** -0.5),
        "conv_w": nrm(ks[5], (Ld, CONV_K_2, M_WIDTH), CONV_K_2 ** -0.5),
        "conv_b": nrm(ks[6], (Ld, M_WIDTH), 0.02),
        "wq_m": nrm(ks[7], (Ld, M_HEADS, M_DV, M_DK), M_DV ** -0.5),
        "wk_m": nrm(ks[8], (Ld, M_HEADS, M_DV, M_DK), M_DV ** -0.5),
        "b_igate": nrm(ks[9], (Ld, M_HEADS), 0.1),
        "b_fgate": b_f,
        "m_out_g": gain(ks[11], (Ld, M_HEADS, M_DV)),
        "cq_norm_g": gain(ks[12], (Ld, Q_LORA)),
        "ckv_norm_g": gain(ks[13], (Ld, KV_LORA)),
        "w_uq": nrm(ks[14], (Ld, Q_LORA, A_HEADS * A_QK), Q_LORA ** -0.5),
        "w_ukv": nrm(ks[15], (Ld, KV_LORA, A_HEADS * (NOPE_DIM + A_DV)), KV_LORA ** -0.5),
        "qk_norm_q": gain(ks[16], (Ld, A_QK)),
        "qk_norm_k": gain(ks[17], (Ld, A_QK)),
        "a_out_g": gain(ks[18], (Ld, A_HEADS, A_DV)),
        "w_out": nrm(ks[19], (Ld, MIX_WIDTH, D_MODEL), MIX_WIDTH ** -0.5),
        "norm_x_g": gain(ks[20], (Ld, D_MODEL)),
        "norm_mem_g": gain(ks[21], (Ld, D_MODEL)),
        "wq_x": nrm(ks[22], (Ld, D_MODEL, X_WIDTH), D_MODEL ** -0.5),
        "wkv_x": nrm(ks[23], (Ld, D_MODEL, 2 * X_WIDTH), D_MODEL ** -0.5),
        "xq_norm_g": gain(ks[24], (Ld, X_HD)),
        "xk_norm_g": gain(ks[25], (Ld, X_HD)),
        "wo_x": nrm(ks[26], (Ld, X_WIDTH, D_MODEL), X_WIDTH ** -0.5),
        "norm_ffn_g": gain(ks[27], (Ld, D_MODEL)),
        "w_ff1": nrm(ks[28], (Ld, D_MODEL, D_FF), D_MODEL ** -0.5),
        "w_ff2": nrm(ks[29], (Ld, D_FF, D_MODEL), D_FF ** -0.5),
    }

def second_block(x, mem, positions, norm_mix_g, w_in, conv_w, conv_b, wq_m, wk_m, b_igate, b_fgate,
              m_out_g, cq_norm_g, ckv_norm_g, w_uq, w_ukv, qk_norm_q, qk_norm_k, a_out_g, w_out,
              norm_x_g, norm_mem_g, wq_x, wkv_x, xq_norm_g, xk_norm_g, wo_x,
              norm_ffn_g, w_ff1, w_ff2):
    cos, sin = rope_tables(positions)
    for l in range(DEPTH_2):
        h = rmsnorm_2(x, norm_mix_g[l])
        x = x + parallel_mixer(h, cos, sin, w_in[l], conv_w[l], conv_b[l], wq_m[l], wk_m[l],
                               b_igate[l], b_fgate[l], m_out_g[l], cq_norm_g[l], ckv_norm_g[l],
                               w_uq[l], w_ukv[l], qk_norm_q[l], qk_norm_k[l], a_out_g[l], w_out[l])
        h = rmsnorm_2(x, norm_x_g[l])
        mem_n = rmsnorm_2(mem, norm_mem_g[l])
        x = x + memory_cross_attention(h, mem_n, wq_x[l], wkv_x[l], xq_norm_g[l], xk_norm_g[l], wo_x[l])
        h = rmsnorm_2(x, norm_ffn_g[l])
        x = x + jnp.square(jax.nn.relu(h @ w_ff1[l])) @ w_ff2[l]
    return x


def setup_inputs(seed=0):
    out = dict(first_inputs(seed))
    for name, value in second_inputs(seed + 1).items():
        if name != "x":
            out[name + "_2"] = value
    return out


def reference(
    x, c, ctx, c_ctx, ada_w, ada_b, norm_mix, norm_ffn, attn_w_in, attn_q_norm, attn_k_norm,
    lam_q1, lam_k1, lam_q2, lam_k2, attn_subln, attn_w_out, conv_w_in, conv_w, conv_w_out,
    router_w, moe_w_gate, moe_w_up, moe_w_down, mem_2, positions_2, norm_mix_g_2, w_in_2,
    conv_w_2, conv_b_2, wq_m_2, wk_m_2, b_igate_2, b_fgate_2, m_out_g_2, cq_norm_g_2,
    ckv_norm_g_2, w_uq_2, w_ukv_2, qk_norm_q_2, qk_norm_k_2, a_out_g_2, w_out_2, norm_x_g_2,
    norm_mem_g_2, wq_x_2, wkv_x_2, xq_norm_g_2, xk_norm_g_2, wo_x_2, norm_ffn_g_2, w_ff1_2,
    w_ff2_2,
):
    x = first_block(
        x, c, ctx, c_ctx, ada_w, ada_b, norm_mix, norm_ffn, attn_w_in, attn_q_norm, attn_k_norm,
        lam_q1, lam_k1, lam_q2, lam_k2, attn_subln, attn_w_out, conv_w_in, conv_w, conv_w_out,
        router_w, moe_w_gate, moe_w_up, moe_w_down,
    )
    return second_block(
        x, mem_2, positions_2, norm_mix_g_2, w_in_2, conv_w_2, conv_b_2, wq_m_2, wk_m_2,
        b_igate_2, b_fgate_2, m_out_g_2, cq_norm_g_2, ckv_norm_g_2, w_uq_2, w_ukv_2,
        qk_norm_q_2, qk_norm_k_2, a_out_g_2, w_out_2, norm_x_g_2, norm_mem_g_2, wq_x_2, wkv_x_2,
        xq_norm_g_2, xk_norm_g_2, wo_x_2, norm_ffn_g_2, w_ff1_2, w_ff2_2,
    )


_drawn_inputs = setup_inputs


def setup_inputs(seed=0):
    import zlib

    import numpy as np

    out = dict(_drawn_inputs(seed))
    spreads = {}
    factors = {'norm_mix': 3.496,
     'norm_ffn': 4.217,
     'attn_q_norm': 8.0,
     'attn_k_norm': 8.0,
     'lam_k1': 4.058,
     'lam_q2': 4.459,
     'lam_k2': 6.682,
     'attn_subln': 5.81,
     'norm_mix_g_2': 2.934,
     'conv_b_2': 5.713,
     'b_igate_2': 197.112,
     'm_out_g_2': 29.011,
     'cq_norm_g_2': 7.738,
     'ckv_norm_g_2': 4.293,
     'qk_norm_q_2': 6.693,
     'qk_norm_k_2': 7.789,
     'a_out_g_2': 18.761,
     'norm_x_g_2': 8.0,
     'norm_mem_g_2': 8.0,
     'xq_norm_g_2': 8.0,
     'xk_norm_g_2': 8.0,
     'norm_ffn_g_2': 13.04}
    for name, (base, spread) in spreads.items():
        noise = np.random.default_rng([zlib.crc32(name.encode()), seed]).standard_normal(out[name].shape)
        drawn = base * np.exp(spread * noise) if base else spread * noise
        out[name] = __import__('jax').numpy.asarray(drawn.astype(out[name].dtype))
    for name, factor in factors.items():
        out[name] = (out[name] * factor).astype(out[name].dtype)
    return out
```

```python
from contextlib import ExitStack

import numpy as np
import concourse.bass as bass
from concourse import mybir

ALU = mybir.AluOpType
ACT = mybir.ActivationFunctionType
AX = mybir.AxisListType.X
F32 = mybir.dt.float32
I32 = mybir.dt.int32

P = 128
D = 1024
SEQ = 256
TT = SEQ // P
KD = D // P
EPS = 1e-6
NEXP = 16
CAP = 2 * SEQ // NEXP
UNIT = 2048
SLOTS = 12
HD = 6
MASKED = -1.0e30
LAM_INIT = 0.8 - 0.6
PI = float(np.pi)

TABLE = {}
_at = 0
for _name, _n in (("ident", 128), ("rank", CAP), ("cos", 128), ("sin", 128),
                  ("dft_cos", 512), ("dft_sin", 512), ("grp_cos", 128), ("grp_nsin", 128),
                  ("inv_freq", 32), ("mask_q", 512), ("mask_k", 512), ("pick", 512), ("pick_ada", 512)):
    TABLE[_name] = (_at, _n)
    _at += _n
TABLE_COLS = _at

ROWS = {}
_at = 0
for _name, _n in (("norm_mix", 16), ("norm_ffn", 16), ("norm_mix_g_2", 8), ("norm_x_g_2", 8),
                  ("norm_mem_g_2", 8), ("norm_ffn_g_2", 8), ("attn_subln", 1), ("conv_w", 24),
                  ("conv_w_2", 16), ("conv_b_2", 4), ("m_out_g_2", 4), ("cq_norm_g_2", 2),
                  ("ckv_norm_g_2", 1), ("a_out_g_2", 4), ("q_nope", 1), ("k_nope", 1),
                  ("xq_norm_g_2", 1), ("xk_norm_g_2", 1)):
    ROWS[_name] = (_at, _n)
    _at += _n
NROWS = _at


def constant_table():
    t = np.zeros((P, TABLE_COLS), np.float32)

    def put(name, a):
        at, n = TABLE[name]
        t[:, at:at + n] = np.asarray(a, np.float64).reshape(-1, n)

    p = np.arange(P)
    put("ident", np.eye(P))
    put("rank", np.tile(np.arange(1, CAP + 1), (P, 1)))
    tok = p[:, None] + P * np.arange(TT)[None, :]
    inv = (np.float32(10000.0) ** (-np.arange(16, dtype=np.float32) / np.float32(16))).astype(np.float32)
    ar = (tok // 64).astype(np.float32)[..., None] * inv
    ac = (tok % 64).astype(np.float32)[..., None] * inv
    put("cos", np.cos(np.concatenate([ar, ar, ac, ac], -1).astype(np.float64)).reshape(P, 128))
    put("sin", np.sin(np.concatenate([-ar, ar, -ac, ac], -1).astype(np.float64)).reshape(P, 128))
    ang = 2 * np.pi * ((tok[..., None] * np.arange(SEQ)) % SEQ) / SEQ
    put("dft_cos", np.cos(ang).reshape(P, 512) / 128.0)
    put("dft_sin", np.sin(ang).reshape(P, 512) / 128.0)
    same = (p[:, None] // 64) == (p[None, :] // 64)
    ang = 2 * np.pi * ((p[:, None] % 64) * (p[None, :] % 64) % 64) / 64
    put("grp_cos", np.where(same, np.cos(ang), 0.0))
    put("grp_nsin", np.where(same, -np.sin(ang), 0.0))
    step = (np.arange(0, 64, 2, dtype=np.float32) / np.float32(64)).astype(np.float32)
    put("inv_freq", np.tile(np.float32(1.0) / (np.float32(10000.0) ** step), (P, 1)))
    other = np.arange(SEQ)
    put("mask_q", np.where(other <= tok[..., None], 0.0, MASKED).reshape(P, 512))
    put("mask_k", np.where(tok[..., None] <= other, 0.0, MASKED).reshape(P, 512))
    pick = np.zeros((P, 4, P))
    for h in range(4):
        pick[h, h] = 1.0
    put("pick", pick.reshape(P, 512))
    pick = np.zeros((P, 4, P))
    for j in range(4):
        pick[32 * j, j] = 1.0
    put("pick_ada", pick.reshape(P, 512))
    return t


class Signal:

    def __init__(self, sem):
        self.sem, self.given, self.taken = sem, 0, {}

    def give(self, ins):
        self.given += 1
        ins.then_inc(self.sem, 1)
        return self.given

    def take(self, eng, n=1):
        self.taken[eng.engine] = self.taken.get(eng.engine, 0) + n
        eng.wait_ge(self.sem, self.taken[eng.engine])


def weight_units(w):
    units = []

    def rows(name, a, first, n):
        for u in range(n):
            src = a[first + 256 * u:first + 256 * u + 256, :].rearrange("(a p) n -> p a n", p=P)
            units.append(((name, u), src, (2, 1024)))

    def cols(name, a, c0, widths, tag=0):
        for u, n in enumerate(widths):
            units.append(((name, tag + u), a[:, c0:c0 + n].rearrange("(k p) n -> p k n", p=P),
                          (a.shape[0] // P, n)))
            c0 += n

    def ada(l, ch):
        rows(f"ada{l}.{ch}", w["ada_w"][l][:, ch * D:(ch + 1) * D], 0, 4)

    for ch in (0, 1):
        ada(0, ch)
    cols("in0", w["attn_w_in"][0], 0, [256] * 10)
    head, proj = units[:-10], units[-10:]
    del units[:]
    for ch in range(2, 6):
        ada(0, ch)
    rest = units[:]
    units[:] = head
    for u in range(10):
        units += [proj[u]] + rest[2 * u:2 * u + 2]
    for ch in range(6):
        ada(1, ch)
    cols("out0", w["attn_w_out"][0], 0, [256] * 4)
    units.append("moe0")
    cols("conv_c", w["conv_w_in"][0], D, [256] * 4)
    cols("conv_u", w["conv_w_in"][0], 2 * D, [256] * 4)
    cols("conv_b", w["conv_w_in"][0], 0, [256] * 4)
    cols("out1", w["conv_w_out"][0], 0, [256] * 4)
    units.append("moe1")
    cols("in2", w["w_in_2"][0], 0, [256] * 6)
    cols("in2", w["w_in_2"][0], 1544, [256, 192], tag=6)
    cols("in2", w["w_in_2"][0], 1536, [8], tag=8)
    units.append((("ukv", 0), w["w_ukv_2"][0], (1, 1024)))
    units.append((("uq", 0), w["w_uq_2"][0].rearrange("(k p) n -> p k n", p=P), (2, 768)))
    cols("out2", w["w_out_2"][0], 0, [256] * 4)
    cols("kvx", w["wkv_x_2"][0], 0, [256] * 4)
    cols("qx", w["wq_x_2"][0], 0, [256] * 2)
    cols("ox", w["wo_x_2"][0], 0, [256] * 4)
    cols("ff1", w["w_ff1_2"][0], 0, [256] * 16)
    rows("ff2", w["w_ff2_2"][0], 0, 16)
    return units


def build(nc, w, out):
    ctx = ExitStack()
    with ctx:
        def sb(name, shape, dt=F32):
            return ctx.enter_context(nc.sbuf_tensor(name, shape, dt))

        def sem(name):
            return ctx.enter_context(nc.semaphore(name))

        ring = sb("ring", [P, SLOTS, UNIT])
        table = sb("table", [P, TABLE_COLS])
        x = sb("x", [P, TT, D])
        xn = sb("xn", [P, TT, D])
        hT = sb("hT", [P, KD, SEQ])
        vec = sb("vec", [P, NROWS])
        cond = sb("cond", [P, KD, 32])
        ada_row = sb("ada_row", [P, 6, 256])
        ada_col = sb("ada_col", [P, 3, 4, KD])
        gain = sb("gain", [P, 2, 3, KD])
        gate = sb("gate", [P, D])
        router = sb("router", [P, 2, KD, NEXP])
        heads64 = sb("heads64", [P, 8, 64])
        wqk_m = sb("wqk_m", [P, 2, 4, 64])
        gate_bias = sb("gate_bias", [4, 2])
        pos_i = sb("pos_i", [P, TT], I32)
        st = sb("st", [P, 256])
        scratch = sb("scratch", [P, 13824])

        def carve(base, kb, *shape, parts=P):
            n = int(np.prod(shape))
            at = int(kb * 256)
            v = base[0:parts, at:at + n]
            if len(shape) == 1:
                return v
            names = "abcd"[:len(shape)]
            return v.rearrange(f"p ({' '.join(names)}) -> p {' '.join(names)}",
                               **{c: s for c, s in zip(names, shape)})

        S = scratch[:, :]
        XN = xn[:, :, :].rearrange("p t d -> p (t d)")
        HT = hT[:, :, :].rearrange("p k s -> p (k s)")
        TB = table[:, :]
        GT = gate[:, :]

        def tab(name, *shape):
            at, n = TABLE[name]
            v = table[:, at:at + n]
            if not shape:
                return v
            names = "abcd"[:len(shape)]
            return v.rearrange(f"p ({' '.join(names)}) -> p {' '.join(names)}",
                               **{c: s for c, s in zip(names, shape)})

        ident = tab("ident")
        vec_rows, cond_rows = carve(S, 8, P), carve(S, 9, P, parts=16)
        cos1, sin1 = tab("cos", TT, 64), tab("sin", TT, 64)
        dft_cos, dft_sin = tab("dft_cos", TT, SEQ), tab("dft_sin", TT, SEQ)
        mask_q, mask_k = tab("mask_q", TT, SEQ), tab("mask_k", TT, SEQ)
        zeros = mask_k[:, 0, P:SEQ]
        pick, pick_ada = tab("pick", 4, P), tab("pick_ada", 4, P)
        st_at = [0]

        def stat(n):
            a = st_at[0]
            st_at[0] += n
            assert st_at[0] <= 250
            return st[:, a:a + n]

        def vcol(name, k=0, n=1):
            at = ROWS[name][0] + k
            return vec[:, at:at + n]

        ctx_n = carve(S, 0, TT, D)
        ctx_raw = carve(S, 10, TT, D)
        hcT = carve(S, 44, KD, SEQ)
        ada_rows = {0: [ada_row[:, 2 * c:2 * c + 2, :] for c in range(3)],
                    1: [carve(S, kb, 2, 256) for kb in (16, 50, 52)]}
        q0, k0, v0 = carve(S, 0, TT, 768), carve(S, 6, 4, 768), carve(S, 18, 4, 768)
        f0 = carve(S, 30, TT, 256)
        k0T, q0T = carve(S, 32, HD, 512), carve(S, 44, HD, SEQ)
        spec, w0T = carve(S, 50, 2, 2, SEQ), carve(S, 6, 2, 4, P)
        tmp_a, tmp_b = carve(XN, 0, 768), carve(XN, 3, 768)
        probs0 = carve(XN, 0, 2, 2, 512)
        o0 = carve(S, 0, TT, 768)
        take_p, take_w = carve(S, 16, TT, NEXP, CAP), carve(S, 20, TT, NEXP, CAP)
        xs = carve(S, 24, KD, CAP)
        w_rep = carve(S, 25, TT, 4, CAP)
        silu_s, act_s = carve(S, 26, 256), carve(S, 27, 256)
        actT = carve(S, 28, 2, P)
        comb = carve(S, 29, SEQ)
        y_s = carve(S, 30, D)
        lgT = carve(S, 34, SEQ, parts=16)
        aff = carve(S, 35, TT, NEXP)
        affT = carve(S, 36, 2, SEQ, parts=16)
        chosen, order = carve(S, 38, SEQ, parts=16), carve(S, 39, SEQ, parts=16)
        order_n = carve(S, 40, TT, NEXP)
        lg_n = carve(S, 40.5, TT, NEXP)
        cgT, cu = carve(S, 0, KD, SEQ), carve(S, 8, KD, SEQ + 2)
        zc, zg = carve(S, 17, KD, SEQ), carve(S, 25, KD, SEQ)
        u_pad, ucT = carve(S, 0, 4, SEQ + 3), carve(S, 5, 4, SEQ)
        vm, og = carve(S, 9, TT, 4, 129), carve(S, 14, TT, 512)
        cq, ckv = carve(S, 18, TT, 256), carve(S, 20, TT, 128)
        kr = carve(S, 21, TT, 64)
        cqT, ckvT = carve(S, 22, 2, SEQ), carve(S, 24, 1, SEQ)
        qa, kv = carve(S, 25, TT, 768), carve(S, 31, TT, 1024)
        qmT, kmT = carve(S, 39, 4, SEQ, parts=64), carve(S, 43, 4, SEQ, parts=64)
        kaT, qaT = carve(S, 47, 4, SEQ), carve(XN, 0, 4, SEQ)
        qrT, krT = carve(GT, 0, 4, SEQ, parts=64), carve(S, 51, SEQ, parts=64)
        hm, oa = carve(S, 0, TT, 512), carve(S, 4, TT, 512)
        decay = carve(XN, 4, 2, SEQ)
        pmT = carve(XN, 6, 2, SEQ)
        g_rows = carve(TB, TABLE["dft_cos"][0] / 256.0, 4, SEQ, parts=4)
        g_rows2 = carve(S, 24, 4, SEQ, parts=4)
        sq_t = carve(S, 20, 2, 512)
        trig = tab("cos", 2, TT, 32)
        trig_t = tab("sin", 2, TT, 32)
        mem_raw, mem_n, memT = carve(S, 0, TT, D), carve(S, 8, TT, D), carve(S, 16, KD, SEQ)
        kx, vx = carve(S, 24, TT, 512), carve(S, 28, TT, 512)
        kxT, qx = carve(S, 32, 4, SEQ), carve(S, 36, TT, 512)
        qxT, ox, oxT = carve(S, 40, 4, SEQ), carve(S, 48, TT, 512), carve(S, 44, 4, SEQ)
        hidT = carve(S, 0, 32, SEQ)

        banks = [ctx.enter_context(nc.psum_tensor(f"bank{b}", [P, 512], F32)) for b in range(8)]

        landed = [sem(f"landed{s}") for s in range(SLOTS)]
        unit_read = sem("unit_read")
        full = [sem(f"full{b}") for b in range(8)]
        free = [sem(f"free{b}") for b in range(8)]
        loads = {n: sem(f"load_{n}") for n in ("table", "ident", "x", "ctx", "rows", "cond", "ada", "ada1", "small", "mem")}
        stored = sem("stored")
        v_step, s_step, p_step = Signal(sem("v_step")), Signal(sem("s_step")), Signal(sem("p_step"))
        signals = {}

        def sig(name):
            if name not in signals:
                signals[name] = Signal(sem(name))
            return signals[name]

        place, turns, nxt, ada_open = {}, [0] * 8, [0], [True]

        def tile(pe, name, bank=None):
            if bank is None:
                if nxt[0] % 8 == 7 and ada_open[0]:
                    nxt[0] += 1
                bank = nxt[0] % 8
                nxt[0] += 1
            if turns[bank]:
                pe.wait_ge(free[bank], turns[bank])
            turns[bank] += 1
            assert name not in place, name
            place[name] = (bank, turns[bank])
            return banks[bank]

        def done(name, ins):
            ins.then_inc(full[place[name][0]], 1)

        def product(eng, name):
            b, n = place[name]
            eng.wait_ge(full[b], n)
            return banks[b]

        def copied(eng, name):
            b, n = place[name]
            eng.wait_ge(free[b], n)

        def empty(eng, name, ins):
            b, n = place[name]
            ins.then_inc(free[b], 1)
            eng.wait_ge(free[b], n)

        units = weight_units(w)
        seat, n_unit = {}, 0
        for u in units:
            if isinstance(u, str):
                seat[u] = n_unit
                n_unit += SLOTS * NEXP
            else:
                seat[u[0]] = n_unit
                n_unit += 1
        release = {}

        def expert_slot(l, s):
            g = seat[f"moe{l}"] + s
            return g % SLOTS, g // SLOTS + 1

        def slot(pe, key, *shape):
            g = seat[key]
            pe.wait_ge(landed[g % SLOTS], 16 * (g // SLOTS + 1))
            a, b = shape
            return ring[:, g % SLOTS, 0:a * b].rearrange("p (a b) -> p a b", a=a)

        reads = [0]

        def unit_done(key, ins):
            reads[0] += 1
            ins.then_inc(unit_read, 1)
            release[seat[key]] = (unit_read, reads[0])

        def unit_done_with(key, name):
            b, n = place[name]
            release[seat[key]] = (full[b], n)

        block = ctx.enter_context(nc.Block())

        MOE_READ = sem("moe_read")
        gathered, xs_scaled = sem("gathered"), sem("xs_scaled")
        xs_ready, rep_ready = sem("xs_ready"), sem("rep_ready")
        rep_turned, comb_ready = sem("rep_turned"), sem("comb_ready")
        silu_ready, act_ready = sem("silu_ready"), sem("act_ready")
        act_turned, actT_ready = sem("act_turned"), sem("actT_ready")
        y_left, y_right, combined = sem("y_left"), sem("y_right"), sem("combined")

        def pe_turn_rows(pe, name, src, n=KD):
            for b in range(n // 2):
                T = tile(pe, f"{name}.{b}")
                for i in range(4):
                    k, t = 2 * b + i // 2, i % 2
                    mm = nc.tensor.transpose(T[:, i * P:(i + 1) * P], src[:, t, k * P:(k + 1) * P], ident)
                done(f"{name}.{b}", mm)

        def pe_natural(pe, key, name, lhs, kk, width, last=True):
            W = slot(pe, key, kk, width)
            T = tile(pe, name)
            for t in range(TT):
                for k in range(kk):
                    mm = nc.tensor.matmul(T[:, t * 256:t * 256 + width], lhs[:, k, t * P:(t + 1) * P],
                                          W[:, k, :], start=(k == 0), stop=(k == kk - 1))
            done(name, mm)
            if last:
                unit_done_with(key, name)

        def pe_turned(pe, key, name, rhs, kk):
            W = slot(pe, key, kk, 256)
            T = tile(pe, name)
            for m in range(2):
                for k in range(kk):
                    mm = nc.tensor.matmul(T[:, m * SEQ:(m + 1) * SEQ], W[:, k, m * P:(m + 1) * P],
                                          rhs[:, k, :], start=(k == 0), stop=(k == kk - 1))
            done(name, mm)
            unit_done_with(key, name)

        def pe_ada(pe, l, ch, u):
            name = f"ada{l}.{ch // 2}"
            if ch % 2 == 0 and u == 0:
                tile(pe, name, bank=7)
            T, c0 = banks[7], (ch % 2) * 256
            W = slot(pe, (f"ada{l}.{ch}", u), 2, D)
            for a in range(2):
                k = 2 * u + a
                for j in range(4):
                    mm = nc.tensor.matmul(T[32 * j:32 * j + 32, c0:c0 + 256], cond[:, k, :],
                                          W[:, a, j * 256:j * 256 + 256], start=(k == 0), stop=(k == 7))
            if u == 3 and ch % 2:
                done(name, mm)
                unit_done_with((f"ada{l}.{ch}", u), name)
            else:
                unit_done((f"ada{l}.{ch}", u), mm)

        def pe_ada_cols(pe, l, n):
            for c in ((0,), (1, 2))[n]:
                copied(pe, f"ada{l}.{c}")
            T = tile(pe, f"adaT{l}.{n}")
            for i in range(4):
                ch, b = 3 * n + i // 2, i % 2
                mm = nc.tensor.transpose(T[:, i * P:(i + 1) * P],
                                         ada_rows[l][ch // 2][:, ch % 2, b * P:(b + 1) * P], ident)
            done(f"adaT{l}.{n}", mm)

        def pe_gate(pe, l, ch):
            for n in range(2):
                T = tile(pe, f"gate{l}.{ch}.{n}")
                for j in range(2):
                    mm = nc.tensor.matmul(T[:, j * 256:j * 256 + 256], pick_ada[:, 2 * n + j, :],
                                          ada_rows[l][ch // 2][:, ch % 2, :], start=True, stop=True)
                done(f"gate{l}.{ch}.{n}", mm)

        def pe_attend(pe, name, n_it, keys, score, value, lag=1):
            def scores(i):
                T = tile(pe, f"{name}s{i}")
                mm = score(T, i)
                done(f"{name}s{i}", mm)

            def turn(i):
                sig(f"{name}_exp").take(pe)
                T = tile(pe, f"{name}p{i}")
                e = att_e[:, i % 2, :]
                for b in range(keys(i)):
                    mm = nc.tensor.transpose(T[:, b * P:(b + 1) * P], e[:, b * P:(b + 1) * P], ident)
                done(f"{name}p{i}", mm)

            def weigh(i):
                copied(pe, f"{name}p{i}")
                T = tile(pe, f"{name}o{i}")
                for b in range(keys(i)):
                    mm = nc.tensor.matmul(T[:, 0:P], att_eT[:, i % 2, b * P:(b + 1) * P], value(i, b),
                                          start=(b == 0), stop=(b == keys(i) - 1))
                done(f"{name}o{i}", mm)

            for i in range(n_it + 2):
                if i < n_it:
                    scores(i)
                if 1 <= i <= n_it:
                    turn(i - 1)
                if i >= 2:
                    weigh(i - 2)

        dc = TABLE["dft_cos"][0] / 256.0
        att_sc, att_e, att_eT = carve(TB, dc, 2, SEQ), carve(TB, dc + 2, 2, SEQ), carve(S, 52, 2, SEQ)

        def pe_moe(pe, l):
            pe_turn_rows_after(pe, f"nf{l}")
            for b in range(4):
                copied(pe, f"nf{l}.{b}")
            T = tile(pe, f"lg{l}")
            for k in range(KD):
                mm = nc.tensor.matmul(T[0:16, 0:SEQ], router[:, l, k, :], hT[:, k, :], start=(k == 0), stop=(k == 7))
            done(f"lg{l}", mm)
            copied(pe, f"lg{l}")
            T = tile(pe, f"lgn{l}")
            for t in range(TT):
                mm = nc.tensor.transpose(T[:, t * 16:t * 16 + 16], lgT[:, t * P:(t + 1) * P], ident[0:16, 0:16])
            done(f"lgn{l}", mm)
            sig("aff_ready").take(pe)
            T = tile(pe, f"affT{l}")
            for t in range(TT):
                mm = nc.tensor.transpose(T[0:16, t * P:(t + 1) * P], aff[:, t, :], ident)
            done(f"affT{l}", mm)
            pe_gate(pe, l, 5)
            for b in range(4):
                T = tile(pe, f"moe_acc{l}.{b}", bank=4 + b)
                mm = nc.tensor.matmul(T[:, :], zeros[:, :], table[:, 0:512], start=True, stop=False,
                                      skip_group_check=True)
                done(f"moe_acc{l}.{b}", mm)
            sig("order_ready").take(pe)
            T = tile(pe, f"ord{l}", bank=0)
            for t in range(TT):
                mm = nc.tensor.transpose(T[:, t * 16:t * 16 + 16], order[:, t * P:(t + 1) * P], ident[0:16, 0:16])
            done(f"ord{l}", mm)
            sig("take_ready").take(pe)
            for b in range(4):
                if turns[b]:
                    pe.wait_ge(free[b], turns[b])
            e0 = NEXP * l
            GU, TR, Y = banks[0], banks[1], banks[2:4]
            with pe.Fori(0, NEXP) as e:
                pe.wait_ge(rep_ready, e + (e0 + 1))
                for t in range(TT):
                    mm = nc.tensor.transpose(TR[:, 256 + t * P:256 + (t + 1) * P],
                                             w_rep[:, t, :, :].rearrange("p j c -> p (j c)"), ident)
                mm.then_inc(rep_turned, 1)
                for k in range(KD):
                    for t in range(TT):
                        mm = nc.tensor.matmul(banks[2][:, k * CAP:(k + 1) * CAP], xn[:, t, k * P:(k + 1) * P],
                                              take_p[:, t, e, :], start=(t == 0), stop=(t == 1))
                mm.then_inc(gathered, 1)
                pe.wait_ge(xs_ready, e + (e0 + 1))
                for m in range(2):
                    for k in range(KD):
                        if k % 2 == 0:
                            s, filled = expert_slot(l, 4 * m + k // 2)
                            pe.wait_ge(landed[s], e * 16 + 16 * filled)
                        for j in range(4):
                            mm = nc.tensor.matmul(
                                GU[32 * j:32 * j + 32, m * 256:(m + 1) * 256], xs[:, k, :],
                                ring[:, s, (k % 2) * D + j * 256:(k % 2) * D + (j + 1) * 256],
                                start=(k == 0), stop=(k == KD - 1))
                        if k % 2:
                            mm.then_inc(MOE_READ, 1)
                pe.wait_ge(act_ready, e + (e0 + 1))
                for b in range(2):
                    mm = nc.tensor.transpose(TR[:, b * P:(b + 1) * P], act_s[:, b * P:(b + 1) * P], ident)
                mm.then_inc(act_turned, 1)
                pe.wait_ge(actT_ready, e + (e0 + 1))
                down = [expert_slot(l, 8 + j) for j in range(4)]
                for s, filled in down:
                    pe.wait_ge(landed[s], e * 16 + 16 * filled)
                for n in range(2):
                    for b in range(2):
                        for j in range(4):
                            mm = nc.tensor.matmul(
                                Y[n][32 * j:32 * j + 32, :], actT[:, b, 32 * j:32 * j + 32],
                                ring[:, down[j][0], b * D + n * 512:b * D + (n + 1) * 512],
                                start=(b == 0), stop=(b == 1))
                            if n == 1 and b == 1:
                                mm.then_inc(MOE_READ, 1)
                pe.wait_ge(comb_ready, e + (e0 + 1))
                pe.wait_ge(y_left, e + (e0 + 1))
                pe.wait_ge(y_right, e + (e0 + 1))
                for t in range(TT):
                    for n in range(2):
                        mm = nc.tensor.matmul(banks[4 + 2 * t + n][:, :], comb[:, t * P:(t + 1) * P],
                                              y_s[:, n * 512:(n + 1) * 512], start=False, stop=False,
                                              skip_group_check=True)
                mm.then_inc(combined, 1)

        def pe_turn_rows_after(pe, name, src=None):
            sig("xn_ready").take(pe)
            pe_turn_rows(pe, name, xn if src is None else src)

        @block.tensor
        def _(pe):
            pe.wait_ge(loads["ident"], 16)
            pe.wait_ge(loads["cond"], 32)
            T = tile(pe, "cond")
            done("cond", nc.tensor.transpose(T[:, 0:16], cond_rows[:, :], ident[0:16, 0:16]))
            copied(pe, "cond")
            for ch in (0, 1):
                for u in range(4):
                    pe_ada(pe, 0, ch, u)
            pe.wait_ge(loads["rows"], 16 * len(ROWS))
            T = tile(pe, "vec")
            done("vec", nc.tensor.transpose(T[:, 0:NROWS], vec_rows[0:NROWS, :], ident[0:NROWS, 0:NROWS]))
            pe_ada_cols(pe, 0, 0)
            pe_turn_rows_after(pe, "nx")
            pe_turn_rows_after(pe, "nc", ctx_n)
            for b in range(4):
                copied(pe, f"nx.{b}")
            for u in range(10):
                with_ctx = 3 <= u < 9
                pe_natural(pe, ("in0", u), f"in0.{u}", hT, KD, 256, last=not with_ctx)
                if with_ctx:
                    if u == 3:
                        for b in range(4):
                            copied(pe, f"nc.{b}")
                    pe_natural(pe, ("in0", u), f"in0c.{u}", hcT, KD, 256)
                if u < 8:
                    for i in (2 * u, 2 * u + 1):
                        pe_ada(pe, 0, 2 + i // 4, i % 4)
            copied(pe, "in0.9")
            pe.wait_ge(loads["table"], 16)
            for i, dft in enumerate((dft_cos, dft_sin)):
                T = tile(pe, f"dft{i}")
                for b in range(2):
                    for t in range(TT):
                        mm = nc.tensor.matmul(T[:, b * SEQ:(b + 1) * SEQ], f0[:, t, b * P:(b + 1) * P], dft[:, t, :],
                                              start=(t == 0), stop=(t == 1))
                done(f"dft{i}", mm)
            copied(pe, "dft0")
            copied(pe, "dft1")
            T = tile(pe, "fourier")
            for b in range(2):
                nc.tensor.matmul(T[:, b * SEQ:(b + 1) * SEQ], tab("grp_cos"), spec[:, 0, b, :], start=True, stop=False)
                mm = nc.tensor.matmul(T[:, b * SEQ:(b + 1) * SEQ], tab("grp_nsin"), spec[:, 1, b, :],
                                      start=False, stop=True)
            done("fourier", mm)
            copied(pe, "fourier")
            pe_ada_cols(pe, 0, 1)
            pe_gate(pe, 0, 2)
            for i in range(6):
                sig("rope_ready").take(pe)
                src = q0[:, i, :] if i < 2 else k0[:, i - 2, :]
                for g in range(2):
                    T = tile(pe, f"qkT{i}.{g}")
                    for h in range(3):
                        mm = nc.tensor.transpose(T[:, h * P:(h + 1) * P],
                                                 src[:, (3 * g + h) * P:(3 * g + h + 1) * P], ident)
                    done(f"qkT{i}.{g}", mm)
            for i in range(6):
                for g in range(2):
                    copied(pe, f"qkT{i}.{g}")

            def scores0(i):
                h, t = i // 2, i % 2
                for m in range(2):
                    T = tile(pe, f"a{i}.{m}")
                    done(f"a{i}.{m}", nc.tensor.matmul(
                        T[:, :], q0T[64 * m:64 * m + 64, h, t * P:(t + 1) * P], k0T[64 * m:64 * m + 64, h, :],
                        start=True, stop=True))

            def turn0(i):
                sig("diff_ready").take(pe)
                T = tile(pe, f"aT{i}")
                for b in range(4):
                    mm = nc.tensor.transpose(T[:, b * P:(b + 1) * P], probs0[:, i % 2, 0, b * P:(b + 1) * P], ident)
                done(f"aT{i}", mm)

            def weigh0(i):
                h = i // 2
                copied(pe, f"aT{i}")
                T = tile(pe, f"ao{i}")
                for b in range(4):
                    mm = nc.tensor.matmul(T[:, 0:P], w0T[:, i % 2, b, :], v0[:, b, h * P:(h + 1) * P],
                                          start=(b == 0), stop=(b == 3))
                done(f"ao{i}", mm)

            for u in range(6, 9):
                copied(pe, f"in0.{u}")
                copied(pe, f"in0c.{u}")
            for i in range(2 * HD + 2):
                if i < 2 * HD:
                    scores0(i)
                if 1 <= i <= 2 * HD:
                    turn0(i - 1)
                if i >= 2:
                    weigh0(i - 2)
                if i < 12:
                    for n in (2 * i, 2 * i + 1):
                        pe_ada(pe, 1, n // 4, n % 4)
            for n in range(2):
                pe_ada_cols(pe, 1, n)
            ada_open[0] = False
            sig("o0_ready").take(pe)
            pe_turn_rows(pe, "o0T", o0, HD)
            for b in range(3):
                copied(pe, f"o0T.{b}")
            for u in range(4):
                pe_natural(pe, ("out0", u), f"out0.{u}", hT, KD, 256)
            pe_moe(pe, 0)
            pe_gate(pe, 1, 2)
            pe_turn_rows_after(pe, "n1")
            for b in range(4):
                copied(pe, f"n1.{b}")
            for part in ("conv_c", "conv_u", "conv_b"):
                for u in range(4):
                    pe_turned(pe, (part, u), f"{part}.{u}", hT, KD)
            for u in range(4):
                copied(pe, f"conv_b.{u}")
            for u in range(4):
                pe_natural(pe, ("out1", u), f"out1.{u}", zg, KD, 256)
            pe_moe(pe, 1)
            pe_turn_rows_after(pe, "n2")
            for b in range(4):
                copied(pe, f"n2.{b}")
            for u in range(2):
                pe_turned(pe, ("in2", u), f"in2.{u}", hT, KD)
            for u in range(2, 8):
                pe_natural(pe, ("in2", u), f"in2.{u}", hT, KD, 256 if u < 7 else 192)
            W = slot(pe, ("in2", 8), KD, 8)
            T = tile(pe, "in2.8")
            for g in range(2):
                for k in range(KD):
                    mm = nc.tensor.matmul(T[0:4, g * SEQ:(g + 1) * SEQ], W[:, k, 4 * g:4 * g + 4], hT[:, k, :],
                                          start=(k == 0), stop=(k == 7))
            done("in2.8", mm)
            unit_done_with(("in2", 8), "in2.8")
            sig("rows_ready").take(pe)
            T = tile(pe, "gcol")
            for i, r in enumerate((3, 1)):
                for t in range(TT):
                    mm = nc.tensor.transpose(T[:, 8 * i + 4 * t:8 * i + 4 * t + 4],
                                             g_rows[:, r, t * P:(t + 1) * P], ident[0:4, 0:4])
            done("gcol", mm)
            sig("lora_ready").take(pe)
            T = tile(pe, "cqT")
            for i in range(4):
                mm = nc.tensor.transpose(T[:, i * P:(i + 1) * P], cq[:, i % 2, (i // 2) * P:(i // 2 + 1) * P], ident)
            done("cqT", mm)
            T = tile(pe, "ckvT")
            for t in range(TT):
                mm = nc.tensor.transpose(T[:, t * P:(t + 1) * P], ckv[:, t, :], ident)
            done("ckvT", mm)
            copied(pe, "ckvT")
            W = slot(pe, ("ukv", 0), 1, D)
            for i in range(4):
                t, n = i // 2, i % 2
                T = tile(pe, f"ukv.{i}")
                done(f"ukv.{i}", nc.tensor.matmul(T[:, :], ckvT[:, 0, t * P:(t + 1) * P],
                                                  W[:, 0, n * 512:(n + 1) * 512], start=True, stop=True))
            unit_done_with(("ukv", 0), "ukv.3")
            copied(pe, "cqT")
            W = slot(pe, ("uq", 0), 2, 768)
            for i in range(4):
                t, n = i // 2, i % 2
                T = tile(pe, f"uq.{i}")
                for k in range(2):
                    mm = nc.tensor.matmul(T[:, 0:384], cqT[:, k, t * P:(t + 1) * P],
                                          W[:, k, n * 384:(n + 1) * 384], start=(k == 0), stop=(k == 1))
                done(f"uq.{i}", mm)
            unit_done_with(("uq", 0), "uq.3")
            for k in range(4):
                sig("uc_ready").take(pe)
            for i, name in enumerate(("qm", "km")):
                for g in range(2):
                    T = tile(pe, f"{name}{g}")
                    for h in range(2):
                        mm = nc.tensor.matmul(T[0:64, h * SEQ:(h + 1) * SEQ], wqk_m[:, i, 2 * g + h, :],
                                              ucT[:, 2 * g + h, :], start=True, stop=True)
                    done(f"{name}{g}", mm)
            for g in range(2):
                copied(pe, f"qm{g}")
                copied(pe, f"km{g}")
            copied(pe, "in2.2")
            copied(pe, "in2.3")
            for h in range(4):
                if h % 2 == 0:
                    T = tile(pe, f"nb{h // 2}")
                    for i in range(2):
                        mm = nc.tensor.matmul(T[:, i * SEQ:(i + 1) * SEQ], pick[0:4, h + i, :], g_rows[:, 2, :],
                                              start=True, stop=True)
                    done(f"nb{h // 2}", mm)
                for s in range(TT):
                    T = tile(pe, f"ms{h}.{s}")
                    done(f"ms{h}.{s}", nc.tensor.matmul(
                        T[:, 0:SEQ], kmT[:, h, s * P:(s + 1) * P], qmT[:, h, :], start=True, stop=True))
                copied(pe, f"ms{h}.0")
                copied(pe, f"ms{h}.1")
                T = tile(pe, f"mo{h}")
                nc.tensor.matmul(T[:, 0:129], pmT[:, 0, 0:P], vm[:, 0, h, :], start=True, stop=True)
                nc.tensor.matmul(T[:, 256:385], pmT[:, 0, P:SEQ], vm[:, 0, h, :], start=True, stop=False)
                mm = nc.tensor.matmul(T[:, 256:385], pmT[:, 1, P:SEQ], vm[:, 1, h, :], start=False, stop=True)
                done(f"mo{h}", mm)
            sig("hm_ready").take(pe)
            pe_turn_rows(pe, "hmT", hm, 4)
            sig("qk_ready").take(pe)
            for i, src in enumerate((qa, kv)):
                hw = 192 if i == 0 else 256
                for g in range(2):
                    T = tile(pe, f"qk2T{i}.{g}")
                    for n in range(4):
                        h, t = 2 * g + n // 2, n % 2
                        mm = nc.tensor.transpose(T[:, n * P:(n + 1) * P], src[:, t, h * hw:h * hw + P], ident)
                    done(f"qk2T{i}.{g}", mm)
            for g in range(2):
                T = tile(pe, f"qrT{g}")
                for n in range(4):
                    h, t = 2 * g + n // 2, n % 2
                    mm = nc.tensor.transpose(T[0:64, n * P:(n + 1) * P], qa[:, t, h * 192 + P:(h + 1) * 192], ident)
                done(f"qrT{g}", mm)
            T = tile(pe, "krT")
            for t in range(TT):
                mm = nc.tensor.transpose(T[0:64, t * P:(t + 1) * P], kr[:, t, :], ident)
            done("krT", mm)
            for n in ("qk2T0.0", "qk2T0.1", "qk2T1.0", "qk2T1.1", "qrT0", "qrT1", "krT"):
                copied(pe, n)

            def score2(T, i):
                h, t = i // 2, i % 2
                n = (t + 1) * P
                nc.tensor.matmul(T[:, 0:n], qaT[:, h, t * P:(t + 1) * P], kaT[:, h, 0:n], start=True, stop=False)
                return nc.tensor.matmul(T[:, 0:n], qrT[:, h, t * P:(t + 1) * P], krT[:, 0:n],
                                        start=False, stop=True)

            pe_attend(pe, "b", 8, lambda i: i % 2 + 1, score2,
                      lambda i, b: kv[:, b, (i // 2) * 256 + P:(i // 2) * 256 + 256])
            sig("oa_ready").take(pe)
            pe_turn_rows(pe, "oaT", oa, 4)
            for n in ("hmT.0", "hmT.1", "oaT.0", "oaT.1"):
                copied(pe, n)
            for u in range(4):
                pe_natural(pe, ("out2", u), f"out2.{u}", hT, KD, 256)
            pe_turn_rows_after(pe, "nm", mem_n)
            for b in range(4):
                copied(pe, f"nm.{b}")
            for u in range(4):
                pe_natural(pe, ("kvx", u), f"kvx.{u}", memT, KD, 256)
            sig("kx_ready").take(pe)
            pe_turn_rows(pe, "kxT", kx, 4)
            pe_turn_rows_after(pe, "n3")
            for b in range(4):
                copied(pe, f"n3.{b}")
            for u in range(2):
                pe_natural(pe, ("qx", u), f"qx.{u}", hT, KD, 256)
            sig("qx_ready").take(pe)
            pe_turn_rows(pe, "qxT", qx, 4)
            for n in ("kxT.0", "kxT.1", "qxT.0", "qxT.1"):
                copied(pe, n)
            pe_attend(pe, "c", 8, lambda i: 2,
                      lambda T, i: nc.tensor.matmul(T[:, 0:SEQ], qxT[:, i // 2, (i % 2) * P:(i % 2 + 1) * P],
                                                    kxT[:, i // 2, :], start=True, stop=True),
                      lambda i, b: vx[:, b, (i // 2) * P:(i // 2 + 1) * P])
            for i in range(8):
                copied(pe, f"co{i}")
            pe_turn_rows(pe, "oxT", ox, 4)
            for b in range(2):
                copied(pe, f"oxT.{b}")
            for u in range(4):
                pe_natural(pe, ("ox", u), f"ox.{u}", oxT, 4, 256)
            pe_turn_rows_after(pe, "n4")
            for b in range(4):
                copied(pe, f"n4.{b}")
            for u in range(16):
                pe_turned(pe, ("ff1", u), f"ff1.{u}", hT, KD)
            T = [tile(pe, f"ff2.{i}") for i in range(4)]
            for u in range(16):
                W = slot(pe, ("ff2", u), 2, D)
                copied(pe, f"ff1.{u}")
                for a in range(2):
                    k = 2 * u + a
                    for t in range(TT):
                        for n in range(2):
                            mm = nc.tensor.matmul(T[2 * t + n][:, :], hidT[:, k, t * P:(t + 1) * P],
                                                  W[:, a, n * 512:(n + 1) * 512], start=(k == 0), stop=(k == 31))
                            if k == 31:
                                done(f"ff2.{2 * t + n}", mm)
                if u < 15:
                    unit_done(("ff2", u), mm)
            release[seat[("ff2", 15)]] = None

        ss = stat(12)
        ss_ctx = stat(2)
        lam = stat(4)
        subln = stat(1)
        nmax, esum = stat(4), stat(4)
        first = stat(4)
        soft = stat(4)
        best = stat(8)
        acol, emj = stat(16), stat(8)
        ss24 = stat(24)
        den = stat(4)
        amax, asum = stat(2), stat(8)
        pos_f = stat(2)
        SC2 = {"b": 192.0 ** -0.5, "c": 128.0 ** -0.5}
        rbuf = carve(S, 32, 2, 2, SEQ)
        ATT = {"b": (lambda i: i % 2 + 1, oa), "c": (lambda i: 2, ox)}

        def modulation(l, sub):
            c = (2 * l, 1, 2 * l)[sub]
            return lambda k: (gain[:, l, sub, k:k + 1], ada_col[:, c, 2 * (sub // 2), k:k + 1])

        def plain(name, k0=0):
            return lambda k: (vcol(name, k - k0), None)

        @block.vector
        def _(v):
            V = nc.vector

            def step(ins):
                v_step.give(ins)
                v.wait_ge(v_step.sem, v_step.given)

            def give(name, ins):
                sig(name).give(ins)
                v.wait_ge(sig(name).sem, sig(name).given)

            def bc(ap, shape):
                return ap.to_broadcast(shape)

            def rms(stats, parts):
                for a, n, width in parts:
                    ins = V.tensor_scalar(stats[:, a:a + n], stats[:, a:a + n], 1.0 / width, EPS, ALU.mult, ALU.add)
                    if (a, n, width) != parts[-1]:
                        step(ins)
                give("mean_ready", ins)
                sig("root_ready").take(v)
                tot = sum(n for _, n, _ in parts)
                step(V.reciprocal(stats[:, 0:tot], stats[:, 0:tot]))

            def norm_rows(src, dst, stats=ss):
                sig("squares_ready").take(v)
                rms(stats, [(0, 2, D)])
                V.tensor_scalar(dst[:, 0, :], src[:, 0, :], stats[:, 0:1], None, ALU.mult)
                give("xn_ready", V.tensor_scalar(dst[:, 1, :], src[:, 1, :], stats[:, 1:2], None, ALU.mult))

            def turned(name, dst, mod, tiles, k0=0):
                for b in tiles:
                    T = product(v, f"{name}.{b}")
                    for i in range(2):
                        k = k0 + 2 * b + i
                        g, s = mod(k)
                        ins = V.tensor_scalar(dst[:, k, :], T[:, i * SEQ:(i + 1) * SEQ], g, s, ALU.mult,
                                              *(() if s is None else (ALU.add,)))
                    empty(v, f"{name}.{b}", ins)

            def group_norm(src, n, width, sq, stats, at):
                step(V.tensor_tensor(sq, src, src, ALU.mult))
                step(V.tensor_reduce(stats[:, at:at + n], sq, AX, ALU.add))

            def head_norm0(src, t, g, rope):
                s3 = src.rearrange("p (h d) -> p h d", d=64)
                a3, b3 = (z.rearrange("p (h d) -> p h d", d=64) for z in (tmp_a, tmp_b))
                group_norm(s3, 12, 64, a3, ss, 0)
                rms(ss, [(0, 12, 64)])
                step(V.tensor_tensor(b3, s3, bc(ss[:, 0:12].unsqueeze(2), [P, 12, 64]), ALU.mult))
                fin = V.tensor_tensor(s3, b3, bc(heads64[:, g:g + 1, :], [P, 12, 64]), ALU.mult)
                if rope:
                    step(fin)
                    step(V.tensor_tensor(a3, s3, bc(cos1[:, t:t + 1, :], [P, 12, 64]), ALU.mult))
                    s5, b5 = (z.rearrange("p (g s d) -> p g s d", s=2, d=16) for z in (src, tmp_b))
                    sn = sin1[:, t, :].rearrange("p (h s d) -> p h s d", s=2, d=16)
                    for s in range(2):
                        for q in range(2):
                            ins = V.tensor_tensor(b5[:, q::2, s, :], s5[:, q::2, 1 - s, :],
                                                  bc(sn[:, q:q + 1, s, :], [P, 12, 16]), ALU.mult)
                    step(ins)
                    fin = V.tensor_tensor(s3, a3, b3, ALU.add)
                give("rope_ready", fin)

            give("cond_clear", V.memset(cond[:, :, :], 0.0))

            def ada(l, c):
                T = product(v, f"ada{l}.{c}")
                row = ada_rows[l][c]
                empty(v, f"ada{l}.{c}", V.tensor_tensor(row, T[:, :].rearrange("p (a n) -> p a n", a=2), row, ALU.add))

            def ada_cols(l, n):
                T = product(v, f"adaT{l}.{n}")[:, :].rearrange("p (q b j r) -> p q b j r", q=2, b=2, j=4)
                for c in range(2 - l):
                    for q in range(2):
                        ins = V.tensor_copy(
                            ada_col[:, 2 * l + c, 2 * n + q, :].rearrange("p (j b) -> p b j", b=2), T[:, q, :, :, c])
                empty(v, f"adaT{l}.{n}", ins)
                for c, sub in (((0, 0), (1, 1)) if n == 0 and l == 0 else ((0, 2 * n),)):
                    ins = V.scalar_tensor_tensor(out=gain[:, l, sub, :], in0=ada_col[:, 2 * l + c, 2 * n + 1, :],
                                                 scalar=1.0, in1=vcol(("norm_mix", "norm_ffn")[n], 8 * l, 8),
                                                 op0=ALU.add, op1=ALU.mult)
                give("gain_ready", ins)

            def residual(name, n, gated, last):
                tmp = carve(XN, 6, TT, 256)
                for u in range(n):
                    T = product(v, f"{name}.{u}")[:, :].rearrange("p (t n) -> p t n", t=2)
                    xs_ = x[:, :, u * 256:(u + 1) * 256]
                    if gated is not None:
                        for c in gated:
                            copied(v, c)
                        gt = gate[:, u * 256:(u + 1) * 256].unsqueeze(1)
                        empty(v, f"{name}.{u}", V.tensor_tensor(tmp, T, bc(gt, [P, 2, 256]), ALU.mult))
                        ins = V.tensor_tensor(xs_, xs_, tmp, ALU.add)
                        if u < n - 1:
                            step(ins)
                    else:
                        ins = V.tensor_tensor(xs_, xs_, T, ALU.add)
                        empty(v, f"{name}.{u}", ins)
                if gated is None:
                    ins = V.tensor_copy(st[:, 255:256], ident[:, 0:1])
                give(last, ins)

            def moe(l):
                norm_rows(x, xn)
                turned(f"nf{l}", hT, modulation(l, 2), (0, 2))
                T = product(v, f"lg{l}")
                empty(v, f"lg{l}", V.tensor_copy(lgT, T[0:16, 0:SEQ]))
                T = product(v, f"lgn{l}")[:, 0:32].rearrange("p (t e) -> p t e", t=2)
                step(V.tensor_reduce(soft[:, 0:2], T, AX, ALU.max))
                empty(v, f"lgn{l}", V.tensor_tensor(lg_n, T, bc(soft[:, 0:2].unsqueeze(2), [P, 2, 16]), ALU.subtract))
                sig("router_in").give(V.tensor_copy(st[:, 254:255], ident[:, 0:1]))
                sig("router_exp").take(v)
                step(V.tensor_reduce(soft[:, 2:4], lg_n, AX, ALU.add))
                step(V.reciprocal(soft[:, 0:2], soft[:, 2:4]))
                give("aff_ready", V.tensor_tensor(aff, lg_n, bc(soft[:, 0:2].unsqueeze(2), [P, 2, 16]), ALU.mult))
                T = product(v, f"affT{l}")
                empty(v, f"affT{l}", V.tensor_copy(affT[:, 0, :], T[0:16, 0:SEQ]))
                for r in range(CAP // 8):
                    step(V.max(best[0:16, :], affT[:, r % 2, :]))
                    step(V.match_replace(affT[:, 1 - r % 2, :], best[0:16, :], affT[:, r % 2, :], -1.0))
                step(V.tensor_scalar(chosen, affT[:, 0, :], 0.0, None, ALU.is_lt))
                step(V.tensor_tensor_scan(affT[:, 1, :], chosen, chosen, 0.0, ALU.add, ALU.bypass))
                give("order_ready", V.tensor_tensor(order, affT[:, 1, :], chosen, ALU.mult))
                T = product(v, f"ord{l}")
                empty(v, f"ord{l}", V.tensor_copy(order_n, T[:, 0:32].rearrange("p (t e) -> p t e", t=2)))
                rank = bc(tab("rank").unsqueeze(1), [P, NEXP, CAP])
                for t in range(TT):
                    ins = V.tensor_tensor(take_p[:, t, :, :], bc(order_n[:, t, :].unsqueeze(2), [P, NEXP, CAP]),
                                          rank, ALU.is_equal)
                give("take_ready", ins)
                for t in range(TT):
                    ins = V.tensor_tensor(take_w[:, t, :, :], take_p[:, t, :, :],
                                          bc(aff[:, t, :].unsqueeze(2), [P, NEXP, CAP]), ALU.mult)
                step(ins)
                e0 = NEXP * l

                def expert(e):
                    first = isinstance(e, int) and l == 0
                    if not first:
                        v.wait_ge(rep_turned, e + e0)
                    for j in range(4):
                        ins = V.tensor_copy(w_rep[:, :, j, :], take_w[:, :, e, :])
                    ins.then_inc(rep_ready, 1)
                    if not first:
                        v.wait_ge(MOE_READ, e * 12 + 12 * e0)
                    v.wait_ge(gathered, e + (e0 + 1))
                    V.tensor_tensor(xs, banks[2][:, 0:256].rearrange("p (k c) -> p k c", k=KD),
                                    bc(gain[:, l, 2, :].unsqueeze(2), [P, KD, CAP]), ALU.mult).then_inc(xs_scaled, 1)
                    v.wait_ge(xs_scaled, e + (e0 + 1))
                    V.tensor_tensor(xs, xs, bc(ada_col[:, 2 * l, 2, :].unsqueeze(2), [P, KD, CAP]),
                                    ALU.add).then_inc(xs_ready, 1)
                    v.wait_ge(rep_turned, e + (e0 + 1))
                    if not first:
                        v.wait_ge(combined, e + e0)
                    V.tensor_copy(comb, banks[1][:, 256:512]).then_inc(comb_ready, 1)
                    v.wait_ge(silu_ready, e + (e0 + 1))
                    v.wait_ge(MOE_READ, e * 12 + (12 * e0 + 8))
                    if not first:
                        v.wait_ge(act_turned, e + e0)
                    V.tensor_tensor(act_s, banks[0][:, 256:512], silu_s, ALU.mult).then_inc(act_ready, 1)
                    v.wait_ge(MOE_READ, e * 12 + (12 * e0 + 12))
                    V.tensor_copy(y_s[:, 512:1024], banks[3][:, :]).then_inc(y_right, 1)

                expert(0)
                with v.Fori(1, NEXP) as e:
                    expert(e)
                for n in range(2):
                    copied(v, f"gate{l}.5.{n}")
                v.wait_ge(combined, e0 + NEXP)
                tmp = carve(XN, 0, 2, 512)
                for b in range(4):
                    t, n = b // 2, b % 2
                    T = banks[4 + b]
                    empty(v, f"moe_acc{l}.{b}", V.tensor_tensor(tmp[:, b % 2, :], T[:, :],
                                                                gate[:, n * 512:(n + 1) * 512], ALU.mult))
                    xs_ = x[:, t, n * 512:(n + 1) * 512]
                    ins = V.tensor_tensor(xs_, xs_, tmp[:, b % 2, :], ALU.add)
                    if b < 3:
                        step(ins)
                give("x_ready", ins)

            v.wait_ge(loads["x"], 16)
            norm_rows(x, xn)
            v.wait_ge(loads["ctx"], 16)
            norm_rows(ctx_raw, ctx_n, ss_ctx)
            v.wait_ge(loads["ada"], 192)
            ada(0, 0)
            T = product(v, "vec")
            empty(v, "vec", V.tensor_copy(vec[:, :], T[:, 0:NROWS]))
            ada_cols(0, 0)
            turned("nx", hT, modulation(0, 0), (0, 2))
            turned("nc", hcT, modulation(0, 1), (0, 2))
            for u in range(9):
                if u in (4, 8):
                    ada(0, u // 4)
                T = product(v, f"in0.{u}")[:, :].rearrange("p (t n) -> p t n", t=2)
                dst = (q0, k0, v0)[u // 3]
                c = (u % 3) * 256
                empty(v, f"in0.{u}", V.tensor_copy(dst[:, 0:2, c:c + 256], T))
                if u == 0:
                    v.wait_ge(loads["small"], 16 * N_SMALL)
                    lt = tmp_a[:, 0:128].rearrange("p (a d) -> p a d", a=2)
                    step(V.tensor_tensor(lt, heads64[:, 4:8:2, :], heads64[:, 5:8:2, :], ALU.mult))
                    give("lam_sum", V.tensor_reduce(lam[:, 0:2], lt, AX, ALU.add))
                    sig("lam_exp").take(v)
                    step(V.tensor_tensor(lam[:, 2:3], lam[:, 1:2], lam[:, 0:1], ALU.subtract))
                    step(V.tensor_scalar(lam[:, 3:4], lam[:, 2:3], -LAM_INIT, None, ALU.add))
                    step(V.tensor_scalar(subln, vcol("attn_subln"), 1.0 - LAM_INIT, None, ALU.mult))
                if u == 2:
                    v.wait_ge(loads["table"], 16)
                    for t in range(TT):
                        head_norm0(q0[:, t, :], t, 0, True)
                if u == 5:
                    for c in range(3, 6):
                        copied(v, f"in0c.{c}")
                    for t in range(4):
                        head_norm0(k0[:, t, :], t, 1, t < 2)
            T = product(v, "dft0")
            empty(v, "dft0", V.tensor_copy(spec[:, 0, :, :].rearrange("p b s -> p (b s)"), T[:, :]))
            ada_cols(0, 1)
            v.wait_ge(loads["ada1"], 192)
            nm, es = (z.rearrange("p (b m) -> p b m", b=2) for z in (nmax, esum))

            def diff_max(i):
                for m in range(2):
                    T = product(v, f"a{i}.{m}")
                    step(V.tensor_reduce(nm[:, i % 2, m:m + 1], T[:, :], AX, ALU.max))
                give("diff_max", V.tensor_scalar(nm[:, i % 2, :], nm[:, i % 2, :], -0.125, None, ALU.mult))

            def diff_weights(i):
                copied(v, f"a{i}.0")
                copied(v, f"a{i}.1")
                e_, s_ = probs0[:, i % 2, :, :], es[:, i % 2, :]
                step(V.reciprocal(first[:, i % 4:i % 4 + 1], s_[:, 0:1]))
                step(V.reciprocal(s_[:, 1:2], s_[:, 1:2]))
                step(V.scalar_tensor_tensor(out=s_[:, 1:2], in0=s_[:, 1:2], scalar=lam[:, 3:4], in1=s_[:, 0:1],
                                            op0=ALU.mult, op1=ALU.mult))
                give("diff_ready", V.scalar_tensor_tensor(out=e_[:, 0, :], in0=e_[:, 1, :], scalar=s_[:, 1:2],
                                                          in1=e_[:, 0, :], op0=ALU.mult, op1=ALU.add))

            def diff_out(i):
                h, t = i // 2, i % 2
                T = product(v, f"ao{i}")
                empty(v, f"ao{i}", V.tensor_scalar(o0[:, t, h * P:(h + 1) * P], T[:, 0:P],
                                                   first[:, i % 4:i % 4 + 1], None, ALU.mult))

            for i in range(2 * HD + 2):
                if i in (4, 8, 12):
                    ada(1, i // 4 - 1)
                if i < 2 * HD:
                    diff_max(i)
                if 1 <= i <= 2 * HD:
                    diff_weights(i - 1)
                if i >= 2:
                    diff_out(i - 2)
            for n in range(2):
                ada_cols(1, n)
            for t in range(TT):
                o3 = o0[:, t, :].rearrange("p (h d) -> p h d", d=P)
                group_norm(o3, HD, P, tmp_a.rearrange("p (h d) -> p h d", d=P), ss, 0)
                rms(ss, [(0, HD, P)])
                ins = V.tensor_tensor(o3, o3, bc(ss[:, 0:HD].unsqueeze(2), [P, HD, P]), ALU.mult)
                if t == 0:
                    step(ins)
            give("o0_ready", ins)
            turned("o0T", hT, lambda k: (subln, None), (0, 2))
            residual("out0", 4, ["gate0.2.0", "gate0.2.1"], "x_ready")
            moe(0)
            norm_rows(x, xn)
            turned("n1", hT, modulation(1, 0), (0, 2))
            V.memset(cu[:, :, 0:1], 0.0)
            step(V.memset(cu[:, :, SEQ + 1:SEQ + 2], 0.0))
            for u in range(4):
                copied(v, f"conv_c.{u}")
                T = product(v, f"conv_u.{u}")[:, :].rearrange("p (t n) -> p t n", t=2)
                empty(v, f"conv_u.{u}", V.tensor_tensor(cu[:, 2 * u:2 * u + 2, 1:SEQ + 1], T,
                                                        cgT[:, 2 * u:2 * u + 2, :], ALU.mult))
                for k in (2 * u, 2 * u + 1):
                    step(V.tensor_scalar(zc[:, k, :], cu[:, k, 0:SEQ], vcol("conv_w", k), None, ALU.mult))
                    for i in (1, 2):
                        step(V.scalar_tensor_tensor(out=zc[:, k, :], in0=cu[:, k, i:i + SEQ],
                                                    scalar=vcol("conv_w", 8 * i + k), in1=zc[:, k, :],
                                                    op0=ALU.mult, op1=ALU.add))
            for u in range(4):
                T = product(v, f"conv_b.{u}")[:, :].rearrange("p (t n) -> p t n", t=2)
                empty(v, f"conv_b.{u}", V.tensor_tensor(zg[:, 2 * u:2 * u + 2, :], T, zc[:, 2 * u:2 * u + 2, :], ALU.mult))
            residual("out1", 4, ["gate1.2.0", "gate1.2.1"], "x_ready")
            moe(1)
            norm_rows(x, xn)
            ang, kf = trig_t[:, 0, :, :], trig_t[:, 1, :, :]
            step(V.tensor_copy(pos_f, pos_i[:, :]))
            for t in range(TT):
                ins = V.tensor_scalar(ang[:, t, :], tab("inv_freq"), pos_f[:, t:t + 1], None, ALU.mult)
            step(ins)
            step(V.tensor_scalar(kf, ang, 1.0 / (2 * PI), 12582912.0, ALU.mult, ALU.add))
            step(V.tensor_scalar(kf, kf, -12582912.0, None, ALU.add))
            for c in TWO_PI:
                step(V.scalar_tensor_tensor(out=ang, in0=kf, scalar=-c, in1=ang, op0=ALU.mult, op1=ALU.add))
            step(V.tensor_scalar(trig[:, 0, :, :], ang, PI / 2, None, ALU.add))
            step(V.tensor_scalar(kf, trig[:, 0, :, :], PI, -2 * PI, ALU.is_gt, ALU.mult))
            step(V.tensor_tensor(trig[:, 0, :, :], trig[:, 0, :, :], kf, ALU.add))
            step(V.tensor_copy(trig[:, 1, :, :], ang))
            give("angle_ready", V.tensor_scalar(trig, trig, 3.1415925, -3.1415925, ALU.min, ALU.max))
            V.memset(u_pad[:, :, 0:3], 0.0)
            step(V.memset(vm[:, :, :, P:P + 1], 1.0))
            turned("n2", hT, plain("norm_mix_g_2"), (0, 2))
            for u in (2, 3):
                T = product(v, f"in2.{u}")[:, :].rearrange("p (t h n) -> p t h n", t=2, h=2)
                for t in range(TT):
                    ins = V.tensor_copy(vm[:, t, 2 * (u - 2):2 * (u - 2) + 2, 0:P], T[:, t, :, :])
                empty(v, f"in2.{u}", ins)
            T = product(v, "in2.6")
            empty(v, "in2.6", V.tensor_copy(cq.rearrange("p t n -> p (t n)"), T[:, :]))
            T = product(v, "in2.7")[:, :].rearrange("p (t n) -> p t n", t=2)
            V.tensor_copy(ckv, T[:, :, 0:P])
            empty(v, "in2.7", V.tensor_copy(kr, T[:, :, P:P + 64]))
            T = product(v, "in2.8")
            F_, I_, N_, A_ = (g_rows[:, i, :] for i in (0, 1, 2, 3))
            r0, r1, r2, r3 = (g_rows2[:, i, :] for i in range(4))
            V.tensor_scalar(F_, T[0:4, SEQ:2 * SEQ], gate_bias[:, 1:2], None, ALU.add)
            empty(v, "in2.8", V.tensor_scalar(I_, T[0:4, 0:SEQ], gate_bias[:, 0:1], None, ALU.add))
            give("absf_ready", V.scalar_tensor_tensor(out=r0, in0=F_, scalar=-1.0, in1=F_, op0=ALU.mult, op1=ALU.max))
            sig("softplus_ready").take(v)
            step(V.scalar_tensor_tensor(out=r3, in0=F_, scalar=0.0, in1=r2, op0=ALU.min, op1=ALU.subtract))
            step(V.tensor_tensor_scan(r0, r3, r3, 0.0, ALU.add, ALU.bypass))
            step(V.tensor_tensor(A_, I_, r0, ALU.subtract))
            step(V.tensor_tensor_scan(N_, A_, A_, 0.0, ALU.max, ALU.bypass))
            give("rows_ready", V.tensor_tensor(I_, r0, N_, ALU.add))
            T = product(v, "gcol")
            empty(v, "gcol", V.tensor_copy(acol, T[:, 0:16]))
            sq2 = carve(XN, 4, 1024)
            sv = sq2[:, 0:512].rearrange("p (t n) -> p t n", t=2)
            group_norm(cq, 2, 256, sv, ss, 0)
            group_norm(ckv, 2, P, sv[:, :, 0:P], ss, 2)
            group_norm(kr, 2, 64, sv[:, :, 0:64], ss, 4)
            rms(ss, [(0, 2, 256), (2, 2, P), (4, 2, 64)])
            V.tensor_tensor(cq, cq, bc(ss[:, 0:2].unsqueeze(2), [P, 2, 256]), ALU.mult)
            V.tensor_tensor(ckv, ckv, bc(ss[:, 2:4].unsqueeze(2), [P, 2, P]), ALU.mult)
            give("lora_ready", V.tensor_tensor(kr, kr, bc(ss[:, 4:6].unsqueeze(2), [P, 2, 64]), ALU.mult))
            step(V.tensor_tensor(kr, kr, bc(heads64[:, 3:4, :], [P, 2, 64]), ALU.mult))
            sig("trig_ready").take(v)

            def rope2(x1, x2, c, s, shape):
                n = int(np.prod(shape[1:]))
                a, b, c_, d = (sq2[:, 256 * i:256 * i + n].rearrange(
                    "p (h d) -> p h d", d=32) for i in range(4))
                V.tensor_tensor(a, x1, c, ALU.mult)
                V.tensor_tensor(b, x2, s, ALU.mult)
                V.tensor_tensor(c_, x2, c, ALU.mult)
                step(V.tensor_tensor(d, x1, s, ALU.mult))
                V.tensor_tensor(x1, a, b, ALU.subtract)
                step(V.tensor_tensor(x2, c_, d, ALU.add))

            rope2(kr[:, :, 0:32], kr[:, :, 32:64], trig[:, 0, :, :], trig[:, 1, :, :], [P, 2, 32])
            T = product(v, "cqT")
            for k in range(2):
                ins = V.tensor_scalar(cqT[:, k, :], T[:, k * SEQ:(k + 1) * SEQ], vcol("cq_norm_g_2", k), None, ALU.mult)
            empty(v, "cqT", ins)
            for k in range(4):
                copied(v, f"in2.{k // 2}")
                step(V.tensor_scalar(ucT[:, k, :], u_pad[:, k, 0:SEQ], vcol("conv_w_2", k), None, ALU.mult))
                for i in (1, 2, 3):
                    ins = V.scalar_tensor_tensor(out=ucT[:, k, :], in0=u_pad[:, k, i:i + SEQ],
                                                 scalar=vcol("conv_w_2", 4 * i + k), in1=ucT[:, k, :],
                                                 op0=ALU.mult, op1=ALU.add)
                    if i < 3:
                        step(ins)
                give("conv_ready", ins)
                T = product(v, f"ukv.{k}") if k < 2 else None
                if k < 2:
                    empty(v, f"ukv.{k}", V.tensor_copy(kv[:, 0, k * 512:(k + 1) * 512], T[:, :]))
            for i in range(2):
                T = product(v, f"uq.{i}")
                empty(v, f"uq.{i}", V.tensor_copy(qa[:, 0, i * 384:(i + 1) * 384], T[:, 0:384]))
            for h in range(4):
                T = product(v, f"nb{h // 2}")[:, (h % 2) * SEQ:(h % 2 + 1) * SEQ]
                for s in range(TT):
                    ins = V.scalar_tensor_tensor(out=decay[:, s, :], in0=T, scalar=-1.0, in1=mask_k[:, s, :],
                                                 op0=ALU.mult, op1=ALU.add)
                if h % 2:
                    empty(v, f"nb{h // 2}", ins)
                    ins = V.tensor_copy(st[:, 253:254], ident[:, 0:1])
                give("decay_in", ins)
                sig("decay_ready").take(v)
                if h:
                    product(v, f"mo{h - 1}")
                for s in range(TT):
                    T = product(v, f"ms{h}.{s}")
                    empty(v, f"ms{h}.{s}", V.scalar_tensor_tensor(
                        out=pmT[:, s, :], in0=T[:, 0:SEQ], scalar=0.125, in1=decay[:, s, :],
                        op0=ALU.mult, op1=ALU.mult))
                T = product(v, f"mo{h}")[:, :].rearrange("p (t n) -> p t n", t=2)
                step(V.tensor_copy(den[:, 2:4], T[:, :, P]))
                step(V.scalar_tensor_tensor(out=den[:, 0:2], in0=den[:, 2:4], scalar=-1.0, in1=den[:, 2:4],
                                            op0=ALU.mult, op1=ALU.max))
                step(V.tensor_tensor(den[:, 0:2], den[:, 0:2], emj[:, h:8:4], ALU.max))
                step(V.reciprocal(den[:, 0:2], den[:, 0:2]))
                for t in range(TT):
                    ins = V.tensor_scalar(hm[:, t, h * P:(h + 1) * P], T[:, t, 0:P], den[:, t:t + 1], None, ALU.mult)
                empty(v, f"mo{h}", ins)

            def norm4(buf, sq):
                for t in range(TT):
                    group_norm(buf[:, t, :].rearrange("p (h d) -> p h d", d=P), 4, P,
                               sq[:, 512 * t:512 * t + 512].rearrange("p (h d) -> p h d", d=P), ss, 4 * t)
                rms(ss, [(0, 8, P)])
                for t in range(TT):
                    b3 = buf[:, t, :].rearrange("p (h d) -> p h d", d=P)
                    ins = V.tensor_tensor(b3, b3, bc(ss[:, 4 * t:4 * t + 4].unsqueeze(2), [P, 4, P]), ALU.mult)
                return ins

            step(norm4(hm, sq2))
            copied(v, "in2.4")
            copied(v, "in2.5")
            give("hm_ready", V.tensor_tensor(hm, hm, og, ALU.mult))
            for n in ("uq.2", "uq.3", "ukv.2", "ukv.3"):
                copied(v, n)
            q4 = qa.rearrange("p t (h d) -> p t h d", d=192)
            k4 = kv.rearrange("p t (h d) -> p t h d", d=256)
            for t in range(TT):
                a3 = sq2[:, 0:512].rearrange("p (h d) -> p h d", d=P)
                group_norm(q4[:, t, :, 0:P], 4, P, a3, ss24, 4 * t)
                group_norm(k4[:, t, :, 0:P], 4, P, a3, ss24, 8 + 4 * t)
                group_norm(q4[:, t, :, P:192], 4, 64, sq2[:, 0:256].rearrange("p (h d) -> p h d", d=64),
                           ss24, 16 + 4 * t)
            rms(ss24, [(0, 16, P), (16, 8, 64)])
            for t in range(TT):
                for z, a in ((q4, 4 * t), (k4, 8 + 4 * t)):
                    V.tensor_tensor(z[:, t, :, 0:P], z[:, t, :, 0:P],
                                    bc(ss24[:, a:a + 4].unsqueeze(2), [P, 4, P]), ALU.mult)
                qr = q4[:, t, :, P:192]
                step(V.tensor_tensor(qr, qr, bc(ss24[:, 16 + 4 * t:20 + 4 * t].unsqueeze(2), [P, 4, 64]), ALU.mult))
                step(V.tensor_tensor(qr, qr, bc(heads64[:, 2:3, :], [P, 4, 64]), ALU.mult))
                rope2(qr[:, :, 0:32], qr[:, :, 32:64], bc(trig[:, 0, t:t + 1, :], [P, 4, 32]),
                      bc(trig[:, 1, t:t + 1, :], [P, 4, 32]), [P, 4, 32])
            give("qk_ready", V.tensor_copy(st[:, 252:253], ident[:, 0:1]))
            turned("hmT", hT, plain("m_out_g_2"), (0,))
            for g in range(2):
                T = product(v, f"qk2T1.{g}")
                empty(v, f"qk2T1.{g}", V.tensor_scalar(kaT[:, 2 * g:2 * g + 2, :].rearrange("p h s -> p (h s)"),
                                                       T[:, :], vcol("k_nope"), None, ALU.mult))
            T = product(v, "krT")
            empty(v, "krT", V.tensor_copy(krT, T[0:64, 0:SEQ]))

            def attend(name):
                keys, dst = ATT[name]

                def maxima(i):
                    n = keys(i) * P
                    T = product(v, f"{name}s{i}")[:, 0:n]
                    if name == "b":
                        empty(v, f"{name}s{i}", V.tensor_tensor(att_sc[:, i % 2, 0:n], T, mask_q[:, i % 2, 0:n], ALU.add))
                        T = att_sc[:, i % 2, 0:n]
                    step(V.tensor_reduce(amax[:, i % 2:i % 2 + 1], T, AX, ALU.max))
                    give(f"{name}_max", V.tensor_scalar(amax[:, i % 2:i % 2 + 1], amax[:, i % 2:i % 2 + 1],
                                                        -SC2[name], None, ALU.mult))

                def sums(i):
                    sig(f"{name}_exp").take(v)
                    step(V.reciprocal(asum[:, i:i + 1], asum[:, i:i + 1]))

                def outs(i):
                    T = product(v, f"{name}o{i}")
                    empty(v, f"{name}o{i}", V.tensor_scalar(dst[:, i % 2, (i // 2) * P:(i // 2 + 1) * P], T[:, 0:P],
                                                            asum[:, i:i + 1], None, ALU.mult))

                for i in range(10):
                    if i < 8:
                        maxima(i)
                    if 1 <= i <= 8:
                        sums(i - 1)
                    if i >= 2:
                        outs(i - 2)

            attend("b")
            give("oa_ready", norm4(oa, sq2))
            turned("oaT", hT, plain("a_out_g_2", 4), (0,), 4)
            v.wait_ge(loads["mem"], 16)
            norm_rows(mem_raw, mem_n)
            residual("out2", 4, None, "x_ready")
            turned("nm", memT, plain("norm_mem_g_2"), (0, 2))
            norm_rows(x, xn)
            for u in range(4):
                T = product(v, f"kvx.{u}")[:, :].rearrange("p (t n) -> p t n", t=2)
                dst, c = (kx, vx)[u // 2], (u % 2) * 256
                empty(v, f"kvx.{u}", V.tensor_copy(dst[:, :, c:c + 256], T))
            sqx = carve(S, 48, 1024)
            give("kx_ready", norm4(kx, sqx))
            turned("kxT", kxT, lambda k: (vcol("xk_norm_g_2"), None), (0,))
            turned("n3", hT, plain("norm_x_g_2"), (0, 2))
            for u in range(2):
                T = product(v, f"qx.{u}")[:, :].rearrange("p (t n) -> p t n", t=2)
                empty(v, f"qx.{u}", V.tensor_copy(qx[:, :, u * 256:u * 256 + 256], T))
            give("qx_ready", norm4(qx, sqx))
            turned("qxT", qxT, lambda k: (vcol("xq_norm_g_2"), None), (0,))
            attend("c")
            T = product(v, "oxT.0")
            empty(v, "oxT.0", V.tensor_copy(oxT[:, 0:2, :].rearrange("p k s -> p (k s)"), T[:, :]))
            residual("ox", 4, None, "x_ready")
            norm_rows(x, xn)
            turned("n4", hT, plain("norm_ffn_g_2"), (0, 2))
            for u in range(16):
                sig("relu_ready").take(v)
                T = product(v, f"ff1.{u}")[:, :].rearrange("p (k s) -> p k s", k=2)
                empty(v, f"ff1.{u}", V.tensor_tensor(hidT[:, 2 * u:2 * u + 2, :], T, rbuf[:, u % 2, :, :], ALU.mult))
            for b in range(4):
                t, n = b // 2, b % 2
                T = product(v, f"ff2.{b}")
                xs_ = x[:, t, n * 512:(n + 1) * 512]
                give("out_ready", V.tensor_tensor(xs_, xs_, T[:, :], ALU.add))

        @block.scalar
        def _(s):
            A = nc.scalar

            def step(ins):
                s_step.give(ins)
                s.wait_ge(s_step.sem, s_step.given)

            def squares(src, junk, stats=ss):
                for t in range(TT):
                    ins = A.activation(junk[:, t, :], src[:, t, :], ACT.Square, accum_out=stats[:, t:t + 1])
                sig("squares_ready").give(ins)
                roots(stats, 2)

            def roots(stats, n):
                sig("mean_ready").take(s)
                sig("root_ready").give(A.activation(stats[:, 0:n], stats[:, 0:n], ACT.Sqrt))

            def turned(name, dst, mod, tiles, k0=0):
                for b in tiles:
                    T = product(s, f"{name}.{b}")
                    for i in range(2):
                        k = k0 + 2 * b + i
                        g, sh = mod(k)
                        src = T[:, i * SEQ:(i + 1) * SEQ]
                        if sh is None:
                            ins = A.activation(dst[:, k, :], src, ACT.Copy, scale=g)
                        else:
                            ins = A.activation(dst[:, k, :], src, ACT.Identity, bias=sh, scale=g)
                    empty(s, f"{name}.{b}", ins)

            def gate_out(l, ch):
                for n in range(2):
                    T = product(s, f"gate{l}.{ch}.{n}")
                    empty(s, f"gate{l}.{ch}.{n}", A.copy(gate[:, n * 512:(n + 1) * 512], T[:, :]))

            def moe(l):
                sig("x_ready").take(s)
                squares(x, xn)
                turned(f"nf{l}", hT, modulation(l, 2), (1, 3))
                sig("router_in").take(s)
                copied(s, f"lgn{l}")
                sig("router_exp").give(A.activation(lg_n, lg_n, ACT.Exp))
                gate_out(l, 5)
                e0 = NEXP * l

                def expert(e):
                    first = isinstance(e, int) and l == 0
                    s.wait_ge(MOE_READ, e * 12 + (12 * e0 + 8))
                    if not first:
                        s.wait_ge(act_ready, e + e0)
                    A.activation(silu_s, banks[0][:, 0:256], ACT.Silu).then_inc(silu_ready, 1)
                    s.wait_ge(act_turned, e + (e0 + 1))
                    A.copy(actT.rearrange("p b c -> p (b c)"), banks[1][:, 0:256]).then_inc(actT_ready, 1)
                    s.wait_ge(MOE_READ, e * 12 + (12 * e0 + 12))
                    if not first:
                        s.wait_ge(combined, e + e0)
                    A.copy(y_s[:, 0:512], banks[2][:, :]).then_inc(y_left, 1)

                expert(0)
                with s.Fori(1, NEXP) as e:
                    expert(e)

            s.dma_start(cond_rows[0:8, :], w["c"].rearrange("a (k p) -> (a k) p", p=P)).then_inc(loads["cond"], 16)
            s.dma_start(cond_rows[8:16, :], w["c_ctx"].rearrange("(k p) -> k p", p=P)).then_inc(loads["cond"], 16)
            s.dma_start(ident, w["constants"][:, 0:P]).then_inc(loads["ident"], 16)
            s.dma_start(x[:, :, :], w["x"][0].rearrange("(t p) d -> p t d", p=P)).then_inc(loads["x"], 16)
            s.dma_start(ctx_raw, w["ctx"][0].rearrange("(t p) d -> p t d", p=P)).then_inc(loads["ctx"], 16)

            def load_ada_bias(l, c, load):
                src = w["ada_b"][l].rearrange("(c j n) -> j c n", c=6, j=4)[:, 2 * c:2 * c + 2, :]
                for j in range(4):
                    s.dma_start(ada_rows[l][c][32 * j:32 * j + 32, :, :],
                                src[j:j + 1].to_broadcast([32, 2, 256])).then_inc(load, 16)

            for c in range(3):
                load_ada_bias(0, c, loads["ada"])

            sig("cond_clear").take(s)
            T = product(s, "cond")
            empty(s, "cond", A.activation(cond[:, :, 0:2].rearrange("p k c -> p c k"),
                                          T[:, 0:16].rearrange("p (c k) -> p c k", c=2), ACT.Silu))
            s.wait_ge(loads["x"], 16)
            squares(x, xn)
            s.wait_ge(loads["ctx"], 16)
            squares(ctx_raw, ctx_n, ss_ctx)
            rest = slice(P, TABLE_COLS)
            s.dma_start(table[:, rest], w["constants"][:, rest]).then_inc(loads["table"], 16)
            sig("gain_ready").take(s)
            turned("nx", hT, modulation(0, 0), (1, 3))
            turned("nc", hcT, modulation(0, 1), (1, 3))
            sig("lam_sum").take(s)
            sig("lam_exp").give(A.activation(lam[:, 0:2], lam[:, 0:2], ACT.Exp))
            for u in range(3, 6):
                T = product(s, f"in0c.{u}")[:, :].rearrange("p (t n) -> p t n", t=2)
                c = (u % 3) * 256
                if u == 3:
                    roots(ss, 12)
                    roots(ss, 12)
                empty(s, f"in0c.{u}", A.copy(k0[:, 2:4, c:c + 256], T))
            for u in range(6, 9):
                T = product(s, f"in0c.{u}")[:, :].rearrange("p (t n) -> p t n", t=2)
                c = (u % 3) * 256
                empty(s, f"in0c.{u}", A.copy(v0[:, 2:4, c:c + 256], T))
                for _ in range((1, 1, 2)[u - 6]):
                    roots(ss, 12)
            T = product(s, "in0.9")[:, :].rearrange("p (t n) -> p t n", t=2)
            empty(s, "in0.9", A.copy(f0, T))
            T = product(s, "dft1")
            empty(s, "dft1", A.copy(spec[:, 1, :, :].rearrange("p b s -> p (b s)"), T[:, :]))
            T = product(s, "fourier")
            empty(s, "fourier", A.copy(hT[:, 6:8, :].rearrange("p k s -> p (k s)"), T[:, :]))
            gate_out(0, 2)
            for i in range(6):
                for g in range(2):
                    T = product(s, f"qkT{i}.{g}")[:, 0:384].rearrange("p (h s) -> p h s", h=3)
                    dst, t = (q0T, i) if i < 2 else (k0T, i - 2)
                    empty(s, f"qkT{i}.{g}", A.copy(dst[:, 3 * g:3 * g + 3, t * P:(t + 1) * P], T))
            for c in range(3):
                load_ada_bias(1, c, loads["ada1"])
            sig("gain_ready").take(s)
            nm, es = (z.rearrange("p (b m) -> p b m", b=2) for z in (nmax, esum))
            for i in range(2 * HD + 1):
                if i < 2 * HD:
                    sig("diff_max").take(s)
                    if i >= 2:
                        product(s, f"aT{i - 2}")
                    for m in range(2):
                        T = product(s, f"a{i}.{m}")
                        empty(s, f"a{i}.{m}", A.activation(probs0[:, i % 2, m, :], T[:, :], ACT.Exp,
                                                           bias=nm[:, i % 2, m:m + 1], scale=0.125,
                                                           accum_out=es[:, i % 2, m:m + 1]))
                if i >= 1:
                    n = i - 1
                    T = product(s, f"aT{n}")
                    if n >= 2:
                        product(s, f"ao{n - 2}")
                    empty(s, f"aT{n}", A.copy(w0T[:, n % 2, :, :].rearrange("p b c -> p (b c)"), T[:, :]))
            sig("gain_ready").take(s, 2)
            roots(ss, HD)
            roots(ss, HD)
            turned("o0T", hT, lambda k: (subln, None), (1,))
            moe(0)
            sig("x_ready").take(s)
            squares(x, xn)
            gate_out(1, 2)
            turned("n1", hT, modulation(1, 0), (1, 3))
            for u in range(4):
                T = product(s, f"conv_c.{u}")
                empty(s, f"conv_c.{u}", A.copy(cgT[:, 2 * u:2 * u + 2, :].rearrange("p k s -> p (k s)"), T[:, :]))
            moe(1)
            sig("x_ready").take(s)
            squares(x, xn)
            sig("angle_ready").take(s)
            sig("trig_ready").give(A.activation(trig, trig, ACT.Sin))
            turned("n2", hT, plain("norm_mix_g_2"), (1, 3))
            for u in range(2):
                T = product(s, f"in2.{u}")[:, :].rearrange("p (k s) -> p k s", k=2)
                empty(s, f"in2.{u}", A.copy(u_pad[:, 2 * u:2 * u + 2, 3:SEQ + 3], T))
            for u in (4, 5):
                T = product(s, f"in2.{u}")[:, :].rearrange("p (t n) -> p t n", t=2)
                empty(s, f"in2.{u}", A.activation(og[:, :, (u - 4) * 256:(u - 3) * 256], T, ACT.Sigmoid))
            sig("absf_ready").take(s)
            step(A.activation(g_rows2[:, 1, :], g_rows2[:, 0, :], ACT.Exp, scale=-1.0))
            sig("softplus_ready").give(A.activation(g_rows2[:, 2, :], g_rows2[:, 1, :], ACT.Ln, bias=1.0))
            copied(s, "gcol")
            step(A.activation(emj, acol[:, 8:16], ACT.Exp, scale=-1.0))
            roots(ss, 6)
            T = product(s, "ckvT")
            empty(s, "ckvT", A.activation(ckvT[:, 0, :], T[:, 0:SEQ], ACT.Copy, scale=vcol("ckv_norm_g_2")))
            for k in (2, 3):
                T = product(s, f"ukv.{k}")
                empty(s, f"ukv.{k}", A.copy(kv[:, 1, (k - 2) * 512:(k - 1) * 512], T[:, :]))
            for i in (2, 3):
                T = product(s, f"uq.{i}")
                empty(s, f"uq.{i}", A.copy(qa[:, 1, (i - 2) * 384:(i - 1) * 384], T[:, 0:384]))
            for k in range(4):
                sig("conv_ready").take(s)
                sig("uc_ready").give(A.activation(ucT[:, k, :], ucT[:, k, :], ACT.Silu, bias=vcol("conv_b_2", k)))
            for name, dst in (("qm", qmT), ("km", kmT)):
                for g in range(2):
                    T = product(s, f"{name}{g}")
                    empty(s, f"{name}{g}", A.copy(dst[:, 2 * g:2 * g + 2, :].rearrange("p h s -> p (h s)"), T[0:64, :]))
            for h in range(4):
                sig("decay_in").take(s)
                for t in range(TT):
                    ins = A.activation(decay[:, t, :], decay[:, t, :], ACT.Exp, bias=acol[:, 4 * t + h:4 * t + h + 1])
                sig("decay_ready").give(ins)
            roots(ss, 8)
            roots(ss24, 24)
            turned("hmT", hT, plain("m_out_g_2"), (1,))
            for g in range(2):
                T = product(s, f"qk2T0.{g}")
                empty(s, f"qk2T0.{g}", A.activation(qaT[:, 2 * g:2 * g + 2, :].rearrange("p h s -> p (h s)"),
                                                    T[:, :], ACT.Copy, scale=vcol("q_nope")))
            for g in range(2):
                T = product(s, f"qrT{g}")
                empty(s, f"qrT{g}", A.copy(qrT[:, 2 * g:2 * g + 2, :].rearrange("p h s -> p (h s)"), T[0:64, :]))

            def attend(name):
                keys, _ = ATT[name]
                for i in range(9):
                    if i < 8:
                        n = keys(i) * P
                        sig(f"{name}_max").take(s)
                        if i >= 2:
                            product(s, f"{name}p{i - 2}")
                        src = att_sc[:, i % 2, 0:n] if name == "b" else banks[place[f"{name}s{i}"][0]][:, 0:n]
                        ins = A.activation(att_e[:, i % 2, 0:n], src, ACT.Exp, bias=amax[:, i % 2:i % 2 + 1],
                                           scale=SC2[name], accum_out=asum[:, i:i + 1])
                        if name == "c":
                            empty(s, f"{name}s{i}", ins)
                            ins = A.copy(st[:, 251:252], ident[:, 0:1])
                        sig(f"{name}_exp").give(ins)
                    if i >= 1:
                        j, n = i - 1, keys(i - 1) * P
                        T = product(s, f"{name}p{j}")
                        if j >= 2:
                            product(s, f"{name}o{j - 2}")
                        empty(s, f"{name}p{j}", A.copy(att_eT[:, j % 2, 0:n], T[:, 0:n]))

            attend("b")
            roots(ss, 8)
            product(s, "oaT.1")
            s.dma_start(mem_raw, w["mem_2"][0].rearrange("(t p) d -> p t d", p=P)).then_inc(loads["mem"], 16)
            turned("oaT", hT, plain("a_out_g_2", 4), (1,), 4)
            s.wait_ge(loads["mem"], 16)
            squares(mem_raw, mem_n)
            turned("nm", memT, plain("norm_mem_g_2"), (1, 3))
            sig("x_ready").take(s)
            squares(x, xn)
            roots(ss, 8)
            turned("kxT", kxT, lambda k: (vcol("xk_norm_g_2"), None), (1,))
            turned("n3", hT, plain("norm_x_g_2"), (1, 3))
            roots(ss, 8)
            turned("qxT", qxT, lambda k: (vcol("xq_norm_g_2"), None), (1,))
            attend("c")
            T = product(s, "oxT.1")
            empty(s, "oxT.1", A.copy(oxT[:, 2:4, :].rearrange("p k s -> p (k s)"), T[:, :]))
            sig("x_ready").take(s)
            squares(x, xn)
            turned("n4", hT, plain("norm_ffn_g_2"), (1, 3))
            for u in range(16):
                T = product(s, f"ff1.{u}")
                if u >= 2:
                    copied(s, f"ff1.{u - 2}")
                sig("relu_ready").give(A.activation(rbuf[:, u % 2, :, :].rearrange("p k s -> p (k s)"), T[:, :], ACT.Relu))

        @block.gpsimd
        def _(g):
            for name, a in ROW_SOURCES(w).items():
                at, n = ROWS[name]
                g.dma_start(vec_rows[at:at + n, :], a).then_inc(loads["rows"], 16)
            small = []
            for i, name in enumerate(("attn_q_norm", "attn_k_norm")):
                small.append((heads64[:, i, :], w[name].to_broadcast([P, 64])))
            for i, name in enumerate(("qk_norm_q_2", "qk_norm_k_2")):
                small.append((heads64[:, 2 + i, :], w[name][:, P:192].to_broadcast([P, 64])))
            for i, name in enumerate(("lam_q1", "lam_k1", "lam_q2", "lam_k2")):
                small.append((heads64[:, 4 + i, :], w[name].to_broadcast([P, 64])))
            for l in range(2):
                small.append((router[:, l, :, :], w["router_w"][l].rearrange("(k p) e -> p k e", p=P)))
            for i, name in enumerate(("wq_m_2", "wk_m_2")):
                small.append((wqk_m[:, i, :, :], w[name][0].rearrange("h d e -> d h e")))
            small.append((gate_bias[:, 0:1], w["b_igate_2"].rearrange("a h -> h a")))
            small.append((gate_bias[:, 1:2], w["b_fgate_2"].rearrange("a h -> h a")))
            small.append((pos_i[:, 0:1], w["positions_2"][:, 0:P].rearrange("a p -> p a")))
            small.append((pos_i[:, 1:2], w["positions_2"][:, P:SEQ].rearrange("a p -> p a")))
            assert len(small) == N_SMALL
            for dst, src in small:
                g.dma_start(dst, src, allow_slow_non_contiguous=True).then_inc(loads["small"], 16)

        @block.sync
        def _(sp):
            def room(g):
                if AHEAD <= g < SLOTS:
                    sp.wait_ge(landed[g - AHEAD], 16)
                if g >= SLOTS and release.get(g - SLOTS) is not None:
                    sp.wait_ge(*release[g - SLOTS])

            sp.wait_ge(loads["cond"], 32)
            sp.wait_ge(loads["ident"], 16)
            for item in units:
                if item in ("moe0", "moe1"):
                    l = int(item[-1])
                    g0, e0 = seat[item], NEXP * l
                    mats = [w[n][l] for n in ("moe_w_gate", "moe_w_up", "moe_w_down")]

                    def load_expert(e, s):
                        rows = mats[s // 4][e, (s % 4) * 256:(s % 4 + 1) * 256, :] if isinstance(e, int) else \
                            mats[s // 4][e][(s % 4) * 256:(s % 4 + 1) * 256, :]
                        q = expert_slot(l, s)[0]
                        sp.dma_start(ring[:, q, :].rearrange("p (a n) -> p a n", a=2),
                                     rows.rearrange("(a p) n -> p a n", p=P)).then_inc(landed[q], 16)

                    for s in range(SLOTS):
                        room(g0 + s)
                        load_expert(0, s)
                    with sp.Fori(1, NEXP) as e:
                        for s in range(SLOTS):
                            sp.wait_ge(MOE_READ, e * 12 + (12 * (e0 - 1) + s + 1))
                            load_expert(e, s)
                    for s in range(SLOTS):
                        release[g0 + SLOTS * (NEXP - 1) + s] = (MOE_READ, 12 * (e0 + NEXP - 1) + s + 1)
                    continue
                key, src, (a, b) = item
                g = seat[key]
                room(g)
                sp.dma_start(ring[:, g % SLOTS, 0:a * b].rearrange("p (a b) -> p a b", a=a),
                             src if len(src.shape) == 3 else src.unsqueeze(1)).then_inc(landed[g % SLOTS], 16)
            sp.wait_ge(sig("out_ready").sem, 4)
            sp.dma_start(out[0].rearrange("(t p) d -> p t d", p=P), x[:, :, :]).then_inc(stored, 16)
            sp.wait_ge(stored, 16)


def _two_pi():
    rest, parts = 2 * np.pi, []
    for bits in (9, 11):
        q = 2.0 ** (np.floor(np.log2(abs(rest))) - bits + 1)
        c = np.floor(rest / q) * q
        parts.append(float(c))
        rest -= c
    return parts + [float(np.float32(rest))]


TWO_PI = _two_pi()
N_SMALL = 16
AHEAD = 3


def ROW_SOURCES(w):
    def rows(a):
        names = "abc"[:len(a.shape) - 1]
        return a.rearrange(f"{' '.join(names)} (k p) -> ({' '.join(names)} k) p", p=P)

    src = {n: rows(w[n]) for n in ROWS if n not in ("q_nope", "k_nope")}
    src["q_nope"] = w["qk_norm_q_2"][:, 0:P]
    src["k_nope"] = w["qk_norm_k_2"][:, 0:P]
    return src


_INS = ["x", "c", "ctx", "c_ctx", "ada_w", "ada_b", "norm_mix", "norm_ffn", "attn_w_in", "attn_q_norm",
        "attn_k_norm", "lam_q1", "lam_k1", "lam_q2", "lam_k2", "attn_subln", "attn_w_out", "conv_w_in",
        "conv_w", "conv_w_out", "router_w", "moe_w_gate", "moe_w_up", "moe_w_down", "mem_2", "positions_2",
        "norm_mix_g_2", "w_in_2", "conv_w_2", "conv_b_2", "wq_m_2", "wk_m_2", "b_igate_2", "b_fgate_2",
        "m_out_g_2", "cq_norm_g_2", "ckv_norm_g_2", "w_uq_2", "w_ukv_2", "qk_norm_q_2", "qk_norm_k_2",
        "a_out_g_2", "w_out_2", "norm_x_g_2", "norm_mem_g_2", "wq_x_2", "wkv_x_2", "xq_norm_g_2",
        "xk_norm_g_2", "wo_x_2", "norm_ffn_g_2", "w_ff1_2", "w_ff2_2"]


def kernel(**inputs):
    import concourse.bacc as bacc
    from concourse.bass_utils import run_bass_kernel_spmd

    nc = bacc.Bacc("TRN2", target_bir_lowering=False, num_devices=1)
    arrays, args = {}, {}
    data = {name: np.ascontiguousarray(inputs[name]) for name in _INS}
    data["constants"] = constant_table()
    for name, a in data.items():
        arrays[f"in_{name}"] = a
        args[name] = nc.dram_tensor(f"in_{name}", a.shape, mybir.dt.from_np(a.dtype), kind="ExternalInput").ap()
    out = nc.dram_tensor("out_0", (1, SEQ, D), F32, kind="ExternalOutput").ap()
    build(nc, args, out)
    result = run_bass_kernel_spmd(nc, [arrays], core_ids=[0])
    return result.results[0]["out_0"]
```
